# Optimizing a Trainium2 kernel written in Bass

```python
import math
import jax, jax.numpy as jnp
from jax import lax
import numpy as np

D_MODEL = 2048
BATCH = 1
SEQ = 256
DEPTH = 1

PLE_DIM = 256
EPS = 1e-6
SSM_EXPAND = 2
D_INNER = SSM_EXPAND * D_MODEL
SSM_HEAD_DIM = 64
SSM_HEADS = D_INNER // SSM_HEAD_DIM
SSM_GROUPS = 8
HEADS_PER_GROUP = SSM_HEADS // SSM_GROUPS
D_STATE = 128
CONV_WIDTH = 4
CHUNK = 128
CONV_DIM = D_INNER + 2 * SSM_GROUPS * D_STATE
D_POOL = D_MODEL
POOL_WINDOWS = (2, 4, 8, 16)
POOL_GROUPS = len(POOL_WINDOWS)
POOL_GROUP_DIM = D_POOL // POOL_GROUPS
D_FF = ((8 * D_MODEL // 3 + 255) // 256) * 256
IN_PROJ_DIM = D_INNER + CONV_DIM + SSM_HEADS + D_POOL + 2 * D_MODEL

kernel_name = "hybrid_ssd_pool_gated_block"

def rmsnorm(x, g):
    xf = x.astype(jnp.float32)
    y = xf * lax.rsqrt(jnp.mean(xf * xf, axis=-1, keepdims=True) + EPS)
    return (y * g.astype(jnp.float32)).astype(x.dtype)

def causal_depthwise_conv(u, w, b):
    c = u.shape[-1]
    out = lax.conv_general_dilated(
        u, w[:, None, :].astype(u.dtype), window_strides=(1,),
        padding=[(CONV_WIDTH - 1, 0)], dimension_numbers=("NWC", "WIO", "NWC"),
        feature_group_count=c)
    return out + b

def ssd_chunked_scan(xh, dt, a, bm, cm):
    bsz, s = xh.shape[:2]
    nc = s // CHUNK

    def to_chunks(t):
        return jnp.moveaxis(t.reshape((bsz, nc, CHUNK) + t.shape[2:]), 1, 0)

    xc, dtc, bc, cc = map(to_chunks, (xh, dt, bm, cm))
    causal = jnp.tril(jnp.ones((CHUNK, CHUNK), dtype=bool))

    def step(state, inp):
        x_q, dt_q, b_q, c_q = inp
        dt_t = jnp.moveaxis(dt_q, 1, -1)
        cum = jnp.cumsum(dt_t * a[None, :, :, None], axis=-1)
        seg = cum[..., :, None] - cum[..., None, :]
        decay = jnp.exp(jnp.where(causal, seg, -jnp.inf))
        cb = jnp.einsum('bign,bjgn->bgij', c_q, b_q)
        w = cb[:, :, None] * decay * dt_t[..., None, :]
        y_intra = jnp.einsum('bgrij,bjgrp->bigrp', w, x_q)
        y_inter = jnp.einsum('bign,bgrpn->bigrp', c_q, state) * jnp.moveaxis(jnp.exp(cum), -1, 1)[..., None]
        to_end = jnp.exp(cum[..., -1:] - cum) * dt_t
        new_state = (state * jnp.exp(cum[..., -1])[..., None, None]
                     + jnp.einsum('bjgn,bgrj,bjgrp->bgrpn', b_q, to_end, x_q))
        return new_state, y_intra + y_inter

    state0 = jnp.zeros((bsz, SSM_GROUPS, HEADS_PER_GROUP, SSM_HEAD_DIM, D_STATE), jnp.float32)
    _, ys = lax.scan(step, state0, (xc, dtc, bc, cc))
    return jnp.moveaxis(ys, 0, 1).reshape(xh.shape)

def mamba2_branch(z, xbc, dt_raw, conv_w, conv_b, dt_bias, a_log, d_skip, ssm_norm_g):
    bsz, s, _ = z.shape
    xbc = jax.nn.silu(causal_depthwise_conv(xbc, conv_w, conv_b))
    xs, bm, cm = jnp.split(xbc, [D_INNER, D_INNER + SSM_GROUPS * D_STATE], axis=-1)
    xh = xs.astype(jnp.float32).reshape(bsz, s, SSM_GROUPS, HEADS_PER_GROUP, SSM_HEAD_DIM)
    bm = bm.astype(jnp.float32).reshape(bsz, s, SSM_GROUPS, D_STATE)
    cm = cm.astype(jnp.float32).reshape(bsz, s, SSM_GROUPS, D_STATE)
    dt = jax.nn.softplus(dt_raw.astype(jnp.float32) + dt_bias.astype(jnp.float32))
    dt = dt.reshape(bsz, s, SSM_GROUPS, HEADS_PER_GROUP)
    a = -jnp.exp(a_log.astype(jnp.float32)).reshape(SSM_GROUPS, HEADS_PER_GROUP)
    dsk = d_skip.astype(jnp.float32).reshape(SSM_GROUPS, HEADS_PER_GROUP)[:, :, None]
    y = ssd_chunked_scan(xh, dt, a, bm, cm) + dsk * xh
    y = y.reshape(bsz, s, D_INNER) * jax.nn.silu(z.astype(jnp.float32))
    yg = y.reshape(bsz, s, SSM_GROUPS, D_INNER // SSM_GROUPS)
    yg = yg * lax.rsqrt(jnp.mean(yg * yg, axis=-1, keepdims=True) + EPS)
    return (yg.reshape(bsz, s, D_INNER) * ssm_norm_g.astype(jnp.float32)).astype(z.dtype)

def multiscale_pool_branch(u, w_pool_grp, pool_scale):
    bsz, s, _ = u.shape
    uf = u.astype(jnp.float32).reshape(bsz, s, POOL_GROUPS, POOL_GROUP_DIM)
    cs = jnp.cumsum(uf, axis=1)
    pos = jnp.arange(1, s + 1, dtype=jnp.float32)
    outs = []
    for gi, win in enumerate(POOL_WINDOWS):
        c = cs[:, :, gi]
        prev = jnp.pad(c, ((0, 0), (win, 0), (0, 0)))[:, :s]
        mean = (c - prev) / jnp.minimum(pos, float(win))[None, :, None]
        outs.append(mean - uf[:, :, gi])
    pooled = jnp.stack(outs, axis=2)
    mixed = jnp.einsum('bsgc,gcd->bsgd', pooled, w_pool_grp.astype(jnp.float32))
    return (mixed.reshape(bsz, s, D_POOL) * pool_scale.astype(jnp.float32)).astype(u.dtype)

def setup_inputs(seed: int = 0) -> dict:
    key = jax.random.key(seed)
    ks = jax.random.split(key, 24)
    f32 = jnp.float32

    def nrm(k, shape, scale):
        return jax.random.normal(k, shape, f32) * scale

    def gain(k, shape):
        return 1.0 + 0.1 * jax.random.normal(k, shape, f32)

    dt0 = jnp.exp(jax.random.uniform(ks[5], (DEPTH, SSM_HEADS), f32, math.log(1e-3), math.log(1e-1)))
    dt_bias = dt0 + jnp.log(-jnp.expm1(-dt0))
    a_log = jnp.log(jax.random.uniform(ks[6], (DEPTH, SSM_HEADS), f32, 1.0, 16.0))
    return {
        "x": nrm(ks[0], (BATCH, SEQ, D_MODEL), 1.0),
        "p": nrm(ks[1], (DEPTH, BATCH, SEQ, PLE_DIM), 1.0),
        "w_in": nrm(ks[2], (DEPTH, D_MODEL, IN_PROJ_DIM), D_MODEL ** -0.5),
        "conv_w": nrm(ks[3], (DEPTH, CONV_WIDTH, CONV_DIM), CONV_WIDTH ** -0.5),
        "conv_b": nrm(ks[4], (DEPTH, CONV_DIM), 0.02),
        "dt_bias": dt_bias,
        "a_log": a_log,
        "d_skip": gain(ks[7], (DEPTH, SSM_HEADS)),
        "ssm_norm_g": gain(ks[8], (DEPTH, D_INNER)),
        "w_ssm_out": nrm(ks[9], (DEPTH, D_INNER, D_MODEL), D_INNER ** -0.5),
        "w_pool_grp": nrm(ks[10], (DEPTH, POOL_GROUPS, POOL_GROUP_DIM, POOL_GROUP_DIM), POOL_GROUP_DIM ** -0.5),
        "pool_scale": gain(ks[11], (DEPTH, D_POOL)),
        "w_pool_out": nrm(ks[12], (DEPTH, D_POOL, D_MODEL), D_POOL ** -0.5),
        "w_mix_out": nrm(ks[13], (DEPTH, D_MODEL, D_MODEL), D_MODEL ** -0.5),
        "g_pre_mix": gain(ks[14], (DEPTH, D_MODEL)),
        "g_post_mix": gain(ks[15], (DEPTH, D_MODEL)),
        "g_pre_ffn": gain(ks[16], (DEPTH, D_MODEL)),
        "g_post_ffn": gain(ks[17], (DEPTH, D_MODEL)),
        "w_ffn_in": nrm(ks[18], (DEPTH, D_MODEL, 2 * D_FF), D_MODEL ** -0.5),
        "w_ffn_out": nrm(ks[19], (DEPTH, D_FF, D_MODEL), D_FF ** -0.5),
        "w_ple_proj": nrm(ks[20], (DEPTH, PLE_DIM, D_MODEL), PLE_DIM ** -0.5),
        "w_ple_gate": nrm(ks[21], (DEPTH, D_MODEL, D_MODEL), D_MODEL ** -0.5),
    }

def reference(x, p, w_in, conv_w, conv_b, dt_bias, a_log, d_skip, ssm_norm_g, w_ssm_out,
              w_pool_grp, pool_scale, w_pool_out, w_mix_out, g_pre_mix, g_post_mix,
              g_pre_ffn, g_post_ffn, w_ffn_in, w_ffn_out, w_ple_proj, w_ple_gate):
    splits = list(np.cumsum([D_INNER, CONV_DIM, SSM_HEADS, D_POOL, D_MODEL]))
    for i in range(DEPTH):
        h = rmsnorm(x, g_pre_mix[i])
        proj = jnp.einsum('bsd,de->bse', h, w_in[i])
        z, xbc, dt_raw, u_pool, gate_ssm, gate_pool = jnp.split(proj, splits, axis=-1)
        y_ssm = mamba2_branch(z, xbc, dt_raw, conv_w[i], conv_b[i], dt_bias[i], a_log[i],
                              d_skip[i], ssm_norm_g[i])
        y_pool = multiscale_pool_branch(u_pool, w_pool_grp[i], pool_scale[i])
        merged = (jax.nn.sigmoid(gate_ssm) * jnp.einsum('bse,ed->bsd', y_ssm, w_ssm_out[i])
                  + jax.nn.sigmoid(gate_pool) * jnp.einsum('bse,ed->bsd', y_pool, w_pool_out[i]))
        mix = jnp.einsum('bsd,de->bse', merged, w_mix_out[i])
        x = x + rmsnorm(mix, g_post_mix[i])
        h2 = rmsnorm(x, g_pre_ffn[i])
        gu = jnp.einsum('bsd,df->bsf', h2, w_ffn_in[i])
        g_ff, u_ff = jnp.split(gu, 2, axis=-1)
        f = jnp.einsum('bsf,fd->bsd', jax.nn.silu(g_ff) * u_ff, w_ffn_out[i])
        x = x + rmsnorm(f, g_post_ffn[i])
        ple = jnp.einsum('bsk,kd->bsd', p[i], w_ple_proj[i])
        x = x + jax.nn.sigmoid(jnp.einsum('bsd,de->bse', x, w_ple_gate[i])) * ple
    return x


_drawn_inputs = setup_inputs


def setup_inputs(seed=0):
    import zlib

    import numpy as np

    out = dict(_drawn_inputs(seed))
    spreads = {}
    factors = {'conv_b': 3.431}
    for name, (base, spread) in spreads.items():
        noise = np.random.default_rng([zlib.crc32(name.encode()), seed]).standard_normal(out[name].shape)
        drawn = base * np.exp(spread * noise) if base else spread * noise
        out[name] = __import__('jax').numpy.asarray(drawn.astype(out[name].dtype))
    for name, factor in factors.items():
        out[name] = (out[name] * factor).astype(out[name].dtype)
    return out
```

```python
from contextlib import ExitStack

import numpy as np

import concourse.bass as bass
from concourse import mybir
from concourse.bass import ds

F32 = mybir.dt.float32
F32R = mybir.dt.float32r
ACT = mybir.ActivationFunctionType
ALU = mybir.AluOpType
AX = mybir.AxisListType

P = 128
T = 256
D = 2048
DI = 4096
GROUPS, HEADS, HD = 8, 8, 64
NH = GROUPS * HEADS
CH = 128
CONV = DI + 2 * GROUPS * CH
TAPS = 4
FF = 5632
PLE = 256
EPS = 1e-6
WINDOWS = (2, 4, 8, 16)
CW = 512
NB = CW // P
KB = D // P
NQ = D // CW
Z0, XBC0, DT0 = 0, DI, DI + CONV
U0 = DT0 + NH
GS0, GP0 = U0 + D, U0 + 2 * D

RING = 4
Q_DT = 0
Q_BC = Q_DT + 1
Q_SSD = Q_BC + 4 * 2
Q_POOL = Q_SSD + GROUPS * 4
Q_PO = Q_POOL + 2 * 5
Q_SO = Q_PO + NQ * 4
Q_MIX = Q_SO + NQ * 6
Q_FF = Q_MIX + NQ * 2
NFF = FF // CW
Q_FO = Q_FF + NFF * 4
FO_UNITS = FF // (2 * P)
Q_PP = Q_FO + NQ * FO_UNITS // 4
Q_PG = Q_PP + 1

C_BC = 0
C_SSD = C_BC + 4
C_POOL = C_SSD + 2 * GROUPS
C_PO = C_POOL + 8
C_SO = C_PO + 2 * NQ
C_MIX = C_SO + 2 * NQ
C_FF = C_MIX + NQ
C_FO = C_FF + 2 * NFF
C_PP = C_FO + NQ
C_PG = C_PP + NQ

V_PRE_MIX, V_POST_MIX, V_PRE_FFN, V_POST_FFN, V_POOL, V_SSM = 0, KB, 2 * KB, 3 * KB, 4 * KB, 5 * KB
N_VECS = 5 * KB + DI // P
NCB = CONV // P

RMS_X, RMS_MIX, RMS_X1, RMS_F = range(4)
DT_STEPS = 12
CONV_STEPS = NB * TAPS
Y_STEPS = NB + 3
POOL_STEPS = NB + 3


class Chain:

    def __init__(self, engine, sem, done=0):
        self.engine, self.sem, self.start, self.n = engine, sem, done, 0

    def step(self, instruction):
        instruction.then_inc(self.sem, 1)
        self.n += 1
        return self.n

    def wait(self, n=None):
        self.engine.wait_ge(self.sem, self.start + (self.n if n is None else n))


def build(nc, x, p, w_in, conv_w, conv_b, dt_bias, a_log, d_skip, ssm_norm_g, w_ssm_out,
          w_pool_grp, pool_scale, w_pool_out, w_mix_out, g_pre_mix, g_post_mix,
          g_pre_ffn, g_post_ffn, w_ffn_in, w_ffn_out, w_ple_proj, w_ple_gate, out):
    w_in, w_ssm_out, w_pool_out, w_mix_out = w_in[0], w_ssm_out[0], w_pool_out[0], w_mix_out[0]
    w_ffn_in, w_ffn_out, w_ple_proj, w_ple_gate = w_ffn_in[0], w_ffn_out[0], w_ple_proj[0], w_ple_gate[0]
    x_rows = x[0].rearrange("(a p) n -> p a n", p=P)
    p_rows = p[0, 0].rearrange("(a p) n -> p a n", p=P)
    out_rows = out[0].rearrange("(a p) n -> p a n", p=P)
    cum_dram = nc.dram_tensor("cum_scratch", (NH, T), F32, kind="Internal").ap()
    xT_dram = nc.dram_tensor("xT_scratch", (P, KB, T), F32, kind="Internal").ap()

    SBUF0 = (nc.sbuf_base + 63) // 64 * 64
    def place(name, shape, dt, kb):
        return nc.alloc_sbuf_tensor_at(name, [P] + shape, dt, offset=SBUF0 + int(kb * 1024)).ap()

    h_hi, h_lo = place("h_hi", [KB, T], F32R, 0), place("h_lo", [KB, T], F32R, 16)
    y_hi, y_lo = place("y_hi", [2 * KB, T], F32R, 32), place("y_lo", [2 * KB, T], F32R, 64)
    x_in = place("x_in", [2, D], F32, 32)
    xT0 = place("xT0", [KB, T], F32, 48)
    sq0 = place("sq0", [2, NB, T], F32, 64)
    hf0 = place("hf0", [2, NB, T], F32, 72)
    vrow = place("vrow", [4, P], F32, 80)
    dsk_row = place("dsk_row", [NH], F32, 82)
    head_col = place("head_col", [4], F32, 82.5)
    std0, rstd0 = place("std0", [T], F32, 83), place("rstd0", [T], F32, 84)
    dt_v, dt_e, dt_u, dt_ln = (place(n, [T], F32, kb) for n, kb in
                               (("dt_v", 85), ("dt_e", 86), ("dt_u", 87), ("dt_ln", 88)))
    dt_r, dt_T, dt_a, cum_T = (place(n, [T], F32, kb) for n, kb in
                               (("dt_r", 89), ("dt_T", 90), ("dt_a", 91), ("cum_T", 92)))
    bc = place("bc", [2 * GROUPS, T], F32, 96)
    decay = place("decay", [HEADS, T], F32, 112)
    xraw = place("xraw", [NB, T], F32, 120)
    xs = place("xs", [NB, T], F32, 124)
    zraw = place("zraw", [NB, T], F32, 128)
    ztanh = place("ztanh", [NB, T], F32, 132)
    xdt = place("xdt", [2, HEADS, HD], F32, 136)
    xend = place("xend", [HEADS, HD], F32, 140)
    state = place("state", [HEADS * HD], F32, 142)
    yg = place("yg", [NB, T], F32, 144)
    ecum = place("ecum", [NB, CH], F32, 148)
    bn = place("bn", [CH], F32, 150)
    cbm = place("cbm", [2, CH], F32, 150.5)
    ysum = place("ysum", [T], F32, 151.5)
    ystd = place("ystd", [T], F32, 152.5)
    mask = place("mask", [CH], F32, 153.5)
    cwb = place("cwb", [(TAPS + 1) * NCB], F32, 154)
    tok_dt = place("tok_dt", [2, NH], F32, 155)
    tok_cum = place("tok_cum", [2, NH], F32, 155.5)
    skip = place("skip", [DI // P], F32, 156)
    to_end = place("to_end", [HEADS], F32, 156.25)
    b_own = place("b_own", [T], F32, 156.5)
    yp_hi, yp_lo = place("yp_hi", [KB, T], F32R, 96), place("yp_lo", [KB, T], F32R, 112)
    uraw = place("uraw", [NB, T], F32, 128)
    csum = place("csum", [NB, 16 + T], F32, 132)
    ptmp = place("ptmp", [NB, T], F32, 136.25)
    pool_hi = place("pool_hi", [2, NB, T], F32R, 140.25)
    pool_lo = place("pool_lo", [2, NB, T], F32R, 148.25)
    mpool = place("mpool", [KB, T], F32, 128)
    gate = place("gate", [NB, T], F32, 144)
    prod = place("prod", [NB, T], F32, 148)
    m_hi, m_lo = place("m_hi", [KB, T], F32R, 96), place("m_lo", [KB, T], F32R, 112)
    act_hi, act_lo = place("act_hi", [FF // P, T], F32R, 32), place("act_lo", [FF // P, T], F32R, 76)
    x_back = place("x_back", [KB, T], F32, 52)
    xT = place("xT", [KB, T], F32, 120)
    fg = place("fg", [KB, T], F32, 136)
    sq1 = place("sq1", [2, NB, T], F32, 32)
    hf1 = place("hf1", [2, NB, T], F32, 40)
    std1, rstd1 = place("std1", [T], F32, 48), place("rstd1", [T], F32, 49)
    std2, rstd2 = place("std2", [T], F32, 50), place("rstd2", [T], F32, 51)
    p_in = place("p_in", [2, PLE], F32, 72)
    pf = place("pf", [2, T], F32, 74)
    p_hi, p_lo = place("p_hi", [2, T], F32R, 152), place("p_lo", [2, T], F32R, 154)
    tg = place("tg", [NB, T], F32, 136)
    graw = place("graw", [NB, T], F32, 140)
    uff = place("uff", [NB, T], F32, 144)
    sq_f = place("sq_f", [2, NB, T], F32, 0)
    ple = place("ple", [KB, T], F32, 32)
    std_f, rstd_f = place("std_f", [T], F32, 48), place("rstd_f", [T], F32, 49)
    tgate = place("tgate", [NB, T], F32, 52)
    o_T = place("o_T", [NB, T], F32, 56)
    o_rows = place("o_rows", [2, D], F32, 60)
    ident = place("ident", [P], F32, 157.5)
    ones = place("ones", [T], F32, 158)
    vecs = place("vecs", [N_VECS], F32, 159)
    inv_n = place("inv_n", [len(WINDOWS), 16], F32, 159.5)
    RING0 = 159.84375
    w_raw = place("w_raw", [RING, 2, CW], F32, RING0)
    w_hi = place("w_hi", [RING, 2, CW], F32R, RING0 + 16)
    w_lo = place("w_lo", [RING, 2, CW], F32R, RING0 + 32)

    ctx = ExitStack()
    with ctx:
        acc = [ctx.enter_context(nc.psum_tensor(f"acc{i}", [P, NB, T], F32)) for i in range(2)]
        bank4 = ctx.enter_context(nc.psum_tensor("bank4", [P, 512], F32))
        bank5 = ctx.enter_context(nc.psum_tensor("bank5", [P, 512], F32))
        pair = ctx.enter_context(nc.psum_tensor("pair", [P, NB, T], F32))

        def sem(name):
            return ctx.enter_context(nc.semaphore(name))

        w_landed = [sem(f"w_landed{i}") for i in range(RING)]
        w_hi_done, w_lo_done = sem("w_hi_done"), sem("w_lo_done")
        unit_used = sem("unit_used")
        acc_taken = sem("acc_taken")
        x_landed = [sem(f"x_landed{i}") for i in range(NQ)]
        vec_landed, consts = sem("vec_landed"), sem("consts")
        vecs_t, vecs_ready = sem("vecs_t"), sem("vecs_ready")
        xt_done, xT_stored = sem("xt_done"), sem("xT_stored")
        sq_ready, sq_used = sem("sq_ready"), sem("sq_used")
        std_ready, rstd_ready = sem("std_ready"), sem("rstd_ready")
        fam = {n: (sem(n + "_f"), sem(n + "_h"), sem(n + "_l"))
               for n in ("op_h", "op_y", "op_pool", "op_yp", "op_m", "op_ff", "op_x2", "op_p")}
        dt_done, dt_steps, dt_exp, dt_log = sem("dt_done"), sem("dt_steps"), sem("dt_exp"), sem("dt_log")
        tok_done, tok_ready, cum_stored, cum_landed = (sem("tok_done"), sem("tok_ready"),
                                                       sem("cum_stored"), sem("cum_landed"))
        conv_acc, conv_tanh, conv_out = sem("conv_acc"), sem("conv_tanh"), sem("conv_out")
        cb_done, cb_taken, bn_taken, b_ready = sem("cb_done"), sem("cb_taken"), sem("bn_taken"), sem("b_ready")
        end_ready, seg_ready, decay_ready, w_ready = sem("end_ready"), sem("seg_ready"), sem("decay_ready"), sem("w_ready")
        xtr_done, xdt_ready, xend_ready = sem("xtr_done"), sem("xdt_ready"), sem("xend_ready")
        state_done, state_ready, y_done = sem("state_done"), sem("state_ready"), sem("y_done")
        y_steps, y_gated, ysq_ready, ysum_ready = sem("y_steps"), sem("y_gated"), sem("ysq_ready"), sem("ysum_ready")
        yss_done, ystd_ready, yrstd_ready = sem("yss_done"), sem("ystd_ready"), sem("yrstd_ready")
        pool_steps, merged = sem("pool_steps"), sem("merged")
        xT_landed, res_steps = sem("xT_landed"), sem("res_steps")
        x1_ready = sem("x1_ready")
        p_landed, pt_done = sem("p_landed"), sem("pt_done")
        gg_ready = sem("gg_ready")
        o_steps, o_ready = sem("o_steps"), sem("o_ready")
        ot_done, rows_ready, out_stored = sem("ot_done"), sem("rows_ready"), sem("out_stored")

        block = ctx.enter_context(nc.Block())

        @block.sync
        def _(sp):
            def unit(q, k, src, cols=CW):
                u = 4 * q + k
                if not (isinstance(u, int) and u < RING):
                    sp.wait_ge(w_lo_done, u - RING + 1)
                dst = w_raw[:, k % RING, :, :].rearrange("p a n -> p (a n)")[:, 0:src.shape[1] * cols]
                sp.dma_start(dst.rearrange("p (k n) -> p k n", n=cols), src).then_inc(w_landed[k % RING], 16)

            def chunk(q, k0, w, col, blocks, row0=0, after=None):
                for k in range(blocks // 2):
                    r = row0 + 2 * P * k
                    unit(q, k0 + k, w[r:r + 2 * P, ds(col, CW)].rearrange("(k p) n -> p k n", p=P))
                    if after:
                        after(k)

            for j in range(NQ):
                sp.dma_start(x_in[:, :, ds(CW * j, CW)], x_rows[:, :, ds(CW * j, CW)]).then_inc(x_landed[j], 16)
            at = 0
            for v in (g_pre_mix, g_post_mix, g_pre_ffn, g_post_ffn, pool_scale, ssm_norm_g):
                n = v.shape[1] // P
                sp.dma_start(vrow[at:at + n, 0, :], v[0].rearrange("(b c) -> b c", c=P)).then_inc(vec_landed, 16)
                at += n
            taps = conv_w[0].rearrange("k (b c) -> (k b) c", c=P)
            for i in range(2):
                sp.dma_start(vrow[0:96, 1 + i, :], taps[96 * i:96 * i + 96, :]).then_inc(vec_landed, 16)
            sp.dma_start(vrow[0:NCB, 3, :], conv_b[0].rearrange("(b c) -> b c", c=P)).then_inc(vec_landed, 16)
            sp.dma_start(head_col[0:NH, 0:1], dt_bias[0].rearrange("(h a) -> h a", a=1)).then_inc(vec_landed, 16)
            sp.dma_start(head_col[0:NH, 1:2], a_log[0].rearrange("(h a) -> h a", a=1)).then_inc(vec_landed, 16)
            sp.dma_start(dsk_row[:, :], d_skip.to_broadcast([P, NH])).then_inc(vec_landed, 16)
            for k in range(4):
                unit(Q_DT, k, w_in[CW * k:CW * k + CW, DT0:DT0 + P].rearrange("(k p) n -> p k n", p=P), P)

            chunk(Q_BC, 0, w_in, XBC0 + DI, KB)
            with sp.Fori(1, 4) as c:
                chunk(Q_BC + 2 * c, 0, w_in, XBC0 + DI + CW * c, KB)

            def group(up, first):
                g, q = up - 1, Q_SSD - 4 + 4 * up
                chunk(q, 0, w_in, XBC0 - CW + CW * up, KB)

                def decays(k):
                    if k == 4:
                        if first:
                            sp.wait_ge(cum_stored, 16)
                        else:
                            sp.wait_ge(y_done, g)
                            sp.wait_ge(y_gated, g)
                        rows = cum_dram[ds(HEADS * g, HEADS), :]
                        sp.dma_start(decay[:, :, :], rows.unsqueeze(0).to_broadcast([P, HEADS, T])).then_inc(cum_landed, 16)
                        for half in range(2):
                            odd = rows.rearrange("(b h) t -> h b t", h=2)[half:half + 1, :, CH:T]
                            sp.dma_start(ecum[HD * half:HD * half + HD, :, :],
                                         odd.to_broadcast([HD, NB, CH])).then_inc(cum_landed, 16)
                chunk(q, 8, w_in, CW * up + (Z0 - CW), KB, after=decays)

            group(1, True)
            with sp.Fori(2, GROUPS + 1) as up:
                group(up, False)

            for h in range(2):
                q = Q_POOL + 5 * h
                for i in range(2):
                    chunk(q, 8 * i, w_in, U0 + CW * (2 * h + i), KB)
                for i in range(2):
                    chunk(q, 16 + 2 * i, w_pool_grp[0, 2 * h + i], 0, NB)

            def gated(q, gate_col, w, up, blocks):
                chunk(q, 0, w_in, gate_col - CW + CW * up, KB)
                chunk(q, 8, w, CW * up - CW, blocks)

            with sp.Fori(1, NQ + 1) as up:
                gated(Q_PO - 4 + 4 * up, GP0, w_pool_out, up, KB)
            with sp.Fori(1, NQ + 1) as up:
                gated(Q_SO - 6 + 6 * up, GS0, w_ssm_out, up, 2 * KB)
            with sp.Fori(0, NQ) as j:
                chunk(Q_MIX + 2 * j, 0, w_mix_out, CW * j, KB)
            sp.wait_ge(unit_used, 4 * Q_MIX)
            sp.wait_ge(xT_stored, 16)
            sp.dma_start(x_back[:, :, :], xT_dram).then_inc(xT_landed, 16)
            sp.dma_start(p_in[:, :, :], p_rows).then_inc(p_landed, 16)
            with sp.Fori(0, NFF) as j:
                chunk(Q_FF + 4 * j, 0, w_ffn_in, CW * j, KB)
                chunk(Q_FF + 4 * j, 8, w_ffn_in, FF + CW * j, KB)
            with sp.Fori(0, 2) as t:
                for i in range(2):
                    chunk(Q_FO + t * (FO_UNITS // 2), FO_UNITS * i, w_ffn_out, CW * (2 * t + i), FF // P)
            for c in range(NQ):
                chunk(Q_PP, c, w_ple_proj, CW * c, 2)
            with sp.Fori(0, NQ) as j:
                chunk(Q_PG + 2 * j, 0, w_ple_gate, CW * j, KB)
            for j in range(NQ):
                sp.wait_ge(rows_ready, j + 1)
                sp.dma_start(out_rows[:, :, ds(CW * j, CW)], o_rows[:, :, ds(CW * j, CW)]).then_inc(out_stored, 16)
            sp.wait_ge(out_stored, 16 * NQ)

        @block.gpsimd
        def _(pool):
            pool.memset(ident[:, :], 0.0).then_inc(consts, 1)
            pool.memset(ones[:, :], 1.0).then_inc(consts, 1)
            pool.memset(mask[:, :], 1.0).then_inc(consts, 1)
            for i, w in enumerate(WINDOWS):
                pool.memset(inv_n[:, i, w - 1:16], 1.0 / w).then_inc(consts, 1)
                for t in range(w - 1):
                    pool.memset(inv_n[:, i, t:t + 1], 1.0 / (t + 1)).then_inc(consts, 1)
            n = 3 + sum(WINDOWS)
            pool.wait_ge(consts, n)
            pool.affine_select(out=ident[:, :], in_=ident[:, :], compare_op=ALU.not_equal, fill=1.0, base=0,
                               pattern=[[-1, P]], channel_multiplier=1).then_inc(consts, 1)
            pool.affine_select(out=mask[:, :], in_=mask[:, :], compare_op=ALU.is_ge, fill=0.0, base=0,
                               pattern=[[1, CH]], channel_multiplier=-1).then_inc(consts, 1)

        N_CONSTS = 3 + sum(WINDOWS) + 2

        @block.tensor
        def _(pe):
            def mm(o, l, r, first, last=True):
                return nc.tensor.matmul(o, lhsT=l, rhs=r, start=first, stop=last, skip_group_check=True)

            def turn(o, i, rows=P):
                return nc.tensor.transpose(o, i, ident[0:rows, 0:rows])

            def product(c, q, k0, blocks, hi, lo, accum, wait_for=None, after=None):
                if not (isinstance(c, int) and c < 2):
                    pe.wait_ge(acc_taken, c - 1)
                units = blocks // 2
                for k in range(units):
                    if wait_for:
                        wait_for(k)
                    pe.wait_ge(w_lo_done, 4 * q + k0 + k + 1)
                    s = (k0 + k) % RING
                    for a in range(2):
                        b = 2 * k + a
                        for n in range(NB):
                            o = accum[:, n, :]
                            wh = w_hi[:, s, a, P * n:P * n + P]
                            wl = w_lo[:, s, a, P * n:P * n + P]
                            mm(o, wh, hi[:, b, :], b == 0 and n % 2 == 0, False)
                            mm(o, wh, lo[:, b, :], False, False)
                            last = mm(o, wl, hi[:, b, :], False, b == blocks - 1)
                    last.then_inc(unit_used, 1)
                    if after:
                        after(k)

            def sum_squares(stage, j, sq, o):
                pe.wait_ge(sq_ready, NQ * stage + j + 1)
                for n in range(NB):
                    last = mm(o, ones[:, 0:P], sq[:, j % 2, n, :], j == 0 and n == 0, j == NQ - 1 and n == NB - 1)
                last.then_inc(sq_used, 1)

            pe.wait_ge(consts, N_CONSTS)
            ss = bank4[:, 0:T]
            for j in range(NQ):
                pe.wait_ge(x_landed[j], 16)
                if j >= 2:
                    pe.wait_ge(sq_ready, j - 1)
                for n in range(NB):
                    for a in range(2):
                        last = turn(acc[j % 2][:, n, P * a:P * a + P], x_in[:, a, CW * j + P * n:CW * j + P * n + P])
                last.then_inc(xt_done, 1)
                if j == 0:
                    pe.wait_ge(vec_landed, 16 * 12)
                    turn(bank5[:, 0:N_VECS], vrow[0:N_VECS, 0, :], N_VECS)
                    turn(bank5[:, N_VECS:N_VECS + 96], vrow[0:96, 1, :], 96)
                    turn(bank5[:, N_VECS + 96:N_VECS + 192], vrow[0:96, 2, :], 96)
                    turn(bank5[:, N_VECS + 192:N_VECS + 240], vrow[0:NCB, 3, :], NCB).then_inc(vecs_t, 1)
                else:
                    sum_squares(RMS_X, j - 1, sq0, ss)
            sum_squares(RMS_X, NQ - 1, sq0, ss)

            dt_raw = bank4[:, T:2 * T]
            for k in range(4):
                pe.wait_ge(fam["op_h"][2], k + 1)
                pe.wait_ge(w_lo_done, k + 1)
                wh = w_hi[:, k, :, :].rearrange("p a n -> p (a n)")
                wl = w_lo[:, k, :, :].rearrange("p a n -> p (a n)")
                for a in range(4):
                    b, c = 4 * k + a, P * a
                    mm(dt_raw, wh[:, c:c + P], h_hi[:, b, :], b == 0, False)
                    mm(dt_raw, wh[:, c:c + P], h_lo[:, b, :], False, False)
                    last = mm(dt_raw, wl[:, c:c + P], h_hi[:, b, :], False, b == KB - 1)
                last.then_inc(unit_used, 1)

            def by_token(k):
                if k == 5:
                    pe.wait_ge(dt_steps, DT_STEPS)
                    for i, t in enumerate((dt_T, cum_T)):
                        for a in range(2):
                            last = turn(bank5[:, P * i + NH * a:P * i + NH * a + NH],
                                        t[0:NH, P * a:P * a + P], NH)
                    last.then_inc(tok_done, 1)

            product(C_BC, Q_BC, 0, KB, h_hi, h_lo, acc[0], after=by_token)
            product(C_BC + 1, Q_BC + 2, 0, KB, h_hi, h_lo, acc[1])
            product(C_BC + 2, Q_BC + 4, 0, KB, h_hi, h_lo, acc[0])
            product(C_BC + 3, Q_BC + 6, 0, KB, h_hi, h_lo, acc[1])

            def scan_turns(p_):
                pe.wait_ge(conv_out, 5 + p_)
                pe.wait_ge(cb_taken, p_ + 1)
                pe.wait_ge(bn_taken, p_ + 1)
                for i, bank in enumerate((bank4, bank5)):
                    for n in range(NB):
                        last = turn(bank[:, P * n:P * n + P], xs[:, n, CH * i:CH * i + CH])
                last.then_inc(xtr_done, 1)

            def intra(p_, i):
                for r in range(HEADS):
                    half, n = r % 2, r // 2
                    last = mm(pair[HD * half:HD * half + HD, n, CH * i:CH * i + CH],
                              xdt[:, i, r, :], decay[:, r, CH * i:CH * i + CH], True)
                return last

            def scan_first(p_):
                pe.wait_ge(xdt_ready, 2 * p_ + 2)
                pe.wait_ge(w_ready, p_ + 1)
                intra(p_, 0)
                pe.wait_ge(xend_ready, p_ + 1)
                mm(bank4[:, :], bn[:, :], xend[:, :, :].rearrange("p h d -> p (h d)"), True).then_inc(state_done, 1)

            def scan_second(p_):
                intra(p_, 1)
                pe.wait_ge(state_ready, p_ + 1)
                for n in range(NB):
                    last = mm(bank5[:, CH * n:CH * n + CH], state[:, P * n:P * n + P],
                              bc[:, ds(GROUPS + p_, 1), CH:T].rearrange("p a t -> p (a t)"), True)
                last.then_inc(y_done, 1)

            def y_squares(p_):
                pe.wait_ge(ysum_ready, p_ + 1)
                mm(pair[:, 0, :], ones[:, 0:P], ysum[:, :], True).then_inc(yss_done, 1)

            def bc_products(g, first):
                pe.wait_ge(b_ready, g + 1)
                if not first:
                    pe.wait_ge(state_ready, g)
                    pe.wait_ge(y_gated, g)
                for i in range(2):
                    tokens = slice(CH * i, CH * i + CH)
                    mm(bank4[:, tokens], b_own[:, tokens],
                       bc[:, ds(GROUPS + g, 1), tokens].rearrange("p a t -> p (a t)"), True)
                turn(bank5[:, 0:CH], b_own[:, 0:CH]).then_inc(cb_done, 1)

            def group(g, c, q, own, lag, srcs=None):
                p_ = g - 1

                def a_side(k):
                    if lag:
                        if k == 2:
                            scan_first(p_)
                        if k == 4:
                            scan_second(p_)

                def b_side(k):
                    if lag and k == 1:
                        y_squares(p_)
                    if own and k == 4:
                        bc_products(g, not lag)

                if lag:
                    scan_turns(p_)
                product(c, q, 0, KB, h_hi, h_lo, acc[0], after=a_side)
                product(c + 1, q, 8, KB, h_hi, h_lo, acc[1], after=b_side)

            group(0, C_SSD, Q_SSD, True, False)
            with pe.Fori(1, GROUPS) as g:
                group(g, C_SSD + 2 * g, Q_SSD + 4 * g, True, True)

            for h in range(2):
                c, q = C_POOL + 4 * h, Q_POOL + 5 * h
                group(GROUPS, c, q, False, h == 0)
                for i in range(2):
                    product(c + 2 + i, q, 16 + 2 * i, NB, pool_hi[:, i], pool_lo[:, i], acc[i],
                            wait_for=lambda k: pe.wait_ge(fam["op_pool"][2], 2 * h + i + 1))

            def yp_quarter(k):
                pe.wait_ge(fam["op_yp"][2], k // 2 + 1)

            with pe.Fori(0, NQ) as j:
                product(C_PO + 2 * j, Q_PO + 4 * j, 0, KB, h_hi, h_lo, acc[0])
                product(C_PO + 1 + 2 * j, Q_PO + 4 * j, 8, KB, yp_hi, yp_lo, acc[1],
                        wait_for=lambda k: k % 2 == 0 and yp_quarter(k))
            pe.wait_ge(fam["op_y"][2], GROUPS)
            with pe.Fori(0, NQ) as j:
                product(C_SO + 2 * j, Q_SO + 6 * j, 0, KB, h_hi, h_lo, acc[0])
                product(C_SO + 1 + 2 * j, Q_SO + 6 * j, 8, 2 * KB, y_hi, y_lo, acc[1])
            for j in range(NQ):
                product(C_MIX + j, Q_MIX + 2 * j, 0, KB, m_hi, m_lo, acc[j % 2],
                        wait_for=lambda k: j == 0 and k % 2 == 0 and pe.wait_ge(fam["op_m"][2], k // 2 + 1),
                        after=lambda k: j > 0 and k == 3 and sum_squares(RMS_MIX, j - 1, sq1, ss))
            sum_squares(RMS_MIX, NQ - 1, sq1, ss)
            for j in range(NQ):
                sum_squares(RMS_X1, j, sq1, bank5[:, 0:T])

            def p_turns(k):
                if k == 3:
                    pe.wait_ge(p_landed, 16)
                    for n in range(2):
                        for a in range(2):
                            last = turn(pair[:, n, P * a:P * a + P], p_in[:, a, P * n:P * n + P])
                    last.then_inc(pt_done, 1)

            product(C_FF, Q_FF, 0, KB, h_hi, h_lo, acc[0], after=p_turns,
                    wait_for=lambda k: k % 2 == 0 and pe.wait_ge(fam["op_h"][2], NQ + k // 2 + 1))
            product(C_FF + 1, Q_FF, 8, KB, h_hi, h_lo, acc[1])
            with pe.Fori(1, NFF) as j:
                product(C_FF + 2 * j, Q_FF + 4 * j, 0, KB, h_hi, h_lo, acc[0])
                product(C_FF + 1 + 2 * j, Q_FF + 4 * j, 8, KB, h_hi, h_lo, acc[1])
            for t in range(2):
                for i in range(2):
                    j = 2 * t + i
                    product(C_FO + j, Q_FO + t * (FO_UNITS // 2), FO_UNITS * i, FF // P, act_hi, act_lo, acc[i],
                            wait_for=lambda k: j == 0 and k % 2 == 0 and pe.wait_ge(fam["op_ff"][2], k // 2 + 1),
                            after=lambda k: j > 0 and k == 3 and sum_squares(RMS_F, j - 1, sq_f, ss))
            sum_squares_last = lambda: sum_squares(RMS_F, NQ - 1, sq_f, ss)
            pe.wait_ge(fam["op_p"][2], 1)
            sum_squares_last()
            for c in range(NQ):
                product(C_PP + c, Q_PP, c, 2, p_hi, p_lo, acc[c % 2])

            def rows_out(j):
                pe.wait_ge(o_ready, j + 1)
                if not (isinstance(j, int) and j == 0):
                    pe.wait_ge(rows_ready, j)
                for a in range(2):
                    for n in range(NB):
                        last = turn(pair[:, 2 * a:2 * a + 2, :].rearrange("p b t -> p (b t)")[:, P * n:P * n + P],
                                    o_T[:, n, P * a:P * a + P])
                last.then_inc(ot_done, 1)

            for j in range(NQ):
                product(C_PG + j, Q_PG + 2 * j, 0, KB, h_hi, h_lo, acc[j % 2],
                        wait_for=lambda k: j == 0 and k % 2 == 0 and pe.wait_ge(fam["op_x2"][2], k // 2 + 1),
                        after=lambda k: j > 0 and k == 3 and rows_out(j - 1))
            rows_out(NQ - 1)

        @block.scalar
        def _(act):
            def f(o, i, fn=ACT.Copy, **kw):
                return nc.scalar.activation(o, i, fn, **kw)

            def hi_units(q, k0, n, after=None, cols=2 * CW):
                for k in range(k0, k0 + n):
                    u = 4 * q + k
                    act.wait_ge(w_landed[k % RING], 16 * (q + k // RING) + 16)
                    if not (isinstance(u, int) and u < RING):
                        act.wait_ge(unit_used, u - RING + 1)
                    src = w_raw[:, k % RING, :, :].rearrange("p a n -> p (a n)")[:, 0:cols]
                    dst = w_hi[:, k % RING, :, :].rearrange("p a n -> p (a n)")[:, 0:cols]
                    f(dst, src).then_inc(w_hi_done, 1)
                    if after:
                        after(k - k0)

            def hi_part(name, n, o, i):
                act.wait_ge(fam[name][0], n)
                f(o, i).then_inc(fam[name][1], 1)

            def summed(q, k_end):
                act.wait_ge(unit_used, 4 * q + k_end)

            def root(stage, o, total, eps):
                act.wait_ge(sq_used, NQ * stage + NQ)
                f(o, total, ACT.Sqrt, scale=1.0 / D, bias=eps).then_inc(std_ready, 1)

            for j in range(NQ):
                act.wait_ge(xt_done, j + 1)
                f(xT0[:, 4 * j:4 * j + 4, :], acc[j % 2][:, :, :])
                if j >= 2:
                    act.wait_ge(sq_used, j - 1)
                f(sq0[:, j % 2], acc[j % 2][:, :, :], ACT.Square).then_inc(sq_ready, 1)
                if j == 0:
                    act.wait_ge(vecs_t, 1)
                    f(vecs[:, :], bank5[:, 0:N_VECS])
                    f(cwb[:, :], bank5[:, N_VECS:N_VECS + (TAPS + 1) * NCB], scale=0.5).then_inc(vecs_ready, 1)
            act.wait_ge(sq_ready, NQ)
            act.dma_start(xT_dram, xT0[:, :, :]).then_inc(xT_stored, 16)
            hi_units(Q_DT, 0, 4, cols=CW)
            root(RMS_X, std0[:, :], bank4[:, 0:T], EPS)
            for j in range(NQ):
                hi_part("op_h", j + 1, h_hi[:, 4 * j:4 * j + 4, :], hf0[:, j % 2])
            f(head_col[0:NH, 2:3], head_col[0:NH, 1:2], ACT.Exp).then_inc(dt_exp, 1)

            def conv_take(n, q, k_end, accum):
                summed(q, k_end)
                if not (isinstance(n, int) and n == 0):
                    act.wait_ge(conv_out, n)
                f(xraw[:, :, :], accum[:, :, :]).then_inc(acc_taken, 1)

            def conv_tanhs(n):
                act.wait_ge(conv_acc, CONV_STEPS * (n + 1))
                f(xraw[:, :, :], xs[:, :, :], ACT.Tanh).then_inc(conv_tanh, 1)

            def softplus(k):
                if k == 4:
                    act.wait_ge(dt_steps, 2)
                    f(dt_e[0:NH, :], dt_r[0:NH, :], ACT.Exp, scale=-1.0).then_inc(dt_exp, 1)
                if k == 5:
                    act.wait_ge(dt_steps, 3)
                    f(dt_ln[0:NH, :], dt_u[0:NH, :], ACT.Ln).then_inc(dt_log, 1)
                if k == 7:
                    act.wait_ge(dt_steps, DT_STEPS)
                    act.dma_start(cum_dram, cum_T[0:NH, :]).then_inc(cum_stored, 16)

            hi_units(Q_BC, 0, 8, after=softplus)
            for c in range(1, 4):
                def conv_before(k):
                    if k == 3:
                        conv_take(c - 1, Q_BC + 2 * c, 0, acc[(c - 1) % 2])
                    if k == 7:
                        conv_tanhs(c - 1)
                hi_units(Q_BC + 2 * c, 0, 8, after=conv_before)

            def scan_part(k, p_, q):
                if k == 0:
                    act.wait_ge(cb_done, p_ + 1)
                    f(bn[:, :], bank5[:, 0:CH]).then_inc(bn_taken, 1)
                if k == 1:
                    act.wait_ge(cum_landed, 48 * (p_ + 1))
                    act.wait_ge(seg_ready, p_ + 1)
                    f(to_end[:, :], to_end[:, :], ACT.Exp)
                    f(ecum[:, :, :], ecum[:, :, :], ACT.Exp)
                    f(decay[:, :, :], decay[:, :, :], ACT.Exp).then_inc(decay_ready, 1)
                if k == 3:
                    summed(q, 0)
                    f(zraw[:, :, :], acc[1][:, :, :])
                    f(ztanh[:, :, :], acc[1][:, :, :], ACT.Tanh, scale=0.5).then_inc(acc_taken, 1)
                if k == 6:
                    act.wait_ge(state_done, p_ + 1)
                    f(state[:, :], bank4[:, :]).then_inc(state_ready, 1)
                if k == 10:
                    act.wait_ge(y_gated, p_ + 1)
                    f(ztanh[:, :, :], yg[:, :, :], ACT.Square).then_inc(ysq_ready, 1)
                if k == 12:
                    act.wait_ge(yss_done, p_ + 1)
                    f(ystd[:, :], pair[:, 0, :], ACT.Sqrt, scale=1.0 / CW, bias=4 * EPS).then_inc(ystd_ready, 1)
                if k == 15:
                    hi_part("op_y", p_ + 1, y_hi[:, ds(4 * p_, 4), :], yg[:, :, :])

            def group(g, lag):
                q = Q_SSD + 4 * g

                def at(k):
                    if lag:
                        scan_part(k, g - 1, q)
                    elif k == 3:
                        conv_take(3, q, 0, acc[1])
                    elif k == 7:
                        conv_tanhs(3)
                    if k == 8:
                        act.wait_ge(conv_out, 4)
                        if lag:
                            act.wait_ge(cb_done, g)
                        f(b_own[:, :], bc[:, ds(g, 1), :].rearrange("p a t -> p (a t)")).then_inc(b_ready, 1)
                    if k == 11:
                        conv_take(4 + g, q, 8, acc[0])
                    if k == 14:
                        conv_tanhs(4 + g)
                hi_units(q, 0, 16, after=at)

            act.wait_ge(xT_stored, 16)
            group(0, False)
            with act.Fori(1, GROUPS) as g:
                group(g, True)

            def yp_take(m, q, k_end, accum):
                summed(q, k_end)
                act.wait_ge(fam["op_pool"][2], 2 * (m // 2) + 2)
                if m % 2:
                    act.wait_ge(fam["op_yp"][2], m)
                for n in range(NB):
                    col = V_POOL + NB * m + n
                    last = f(uraw[:, n, :], accum[:, n, :], scale=vecs[:, col:col + 1])
                last.then_inc(acc_taken, 1)
                act.wait_ge(acc_taken, C_POOL + 4 * (m // 2) + 2 + m % 2 + 1)
                f(yp_hi[:, NB * m:NB * m + NB, :], uraw[:, :, :]).then_inc(fam["op_yp"][1], 1)

            for h in range(2):
                q = Q_POOL + 5 * h

                def at(k):
                    if h == 0:
                        scan_part(k, GROUPS - 1, q)
                    else:
                        if k == 1:
                            yp_take(0, q, -2, acc[0])
                        if k == 4:
                            yp_take(1, q, 0, acc[1])
                    if k == 11:
                        summed(q, 8)
                        act.wait_ge(y_gated, GROUPS)
                        if h:
                            act.wait_ge(fam["op_yp"][2], 2)
                        f(uraw[:, :, :], acc[0][:, :, :]).then_inc(acc_taken, 1)
                hi_units(q, 0, 16, after=at)
                if h == 0:
                    act.wait_ge(fam["op_y"][2], GROUPS)
                hi_part("op_pool", 2 * h + 1, pool_hi[:, 0], ptmp[:, :, :])
                hi_units(q, 16, 4)
                summed(q, 16)
                f(uraw[:, :, :], acc[1][:, :, :]).then_inc(acc_taken, 1)
                hi_part("op_pool", 2 * h + 2, pool_hi[:, 1], ptmp[:, :, :])

            def gate_take(m, q):
                summed(q, 8)
                if not (isinstance(m, int) and m == 0):
                    act.wait_ge(merged, m)
                f(gate[:, :, :], acc[0][:, :, :], ACT.Tanh, scale=0.5).then_inc(acc_taken, 1)

            def prod_take(m, q):
                summed(q, 0)
                f(prod[:, :, :], acc[1][:, :, :]).then_inc(acc_taken, 1)

            def po(j, q, first):
                def at(k):
                    if first and k == 1:
                        yp_take(2, q, -2, acc[0])
                    if first and k == 4:
                        yp_take(3, q, 0, acc[1])
                    if not first and k == 3:
                        prod_take(j - 1, q)
                    if k == 11:
                        gate_take(j, q)
                hi_units(q, 0, 16, after=at)

            po(0, Q_PO, True)
            with act.Fori(1, NQ) as j:
                po(j, Q_PO + 4 * j, False)

            def so(j, q, first):
                def at(k):
                    if k == 3:
                        prod_take(NQ + j - 1, q)
                    if k == 6 and not first:
                        hi_part("op_m", j, m_hi[:, ds(4 * (j - 1), 4), :], prod[:, :, :])
                    if k == 11:
                        gate_take(NQ + j, q)
                hi_units(q, 0, 24, after=at)

            so(0, Q_SO, True)
            with act.Fori(1, NQ) as j:
                so(j, Q_SO + 6 * j, False)

            def post_take(stage, j, q, k_end, accum, squares, gain):
                summed(q, k_end)
                if j >= 2:
                    act.wait_ge(sq_used, NQ * stage + j - 1)
                f(squares[:, j % 2], accum[:, :, :], ACT.Square).then_inc(sq_ready, 1)
                for n in range(NB):
                    col = gain + NB * j + n
                    last = f(fg[:, NB * j + n, :], accum[:, n, :], scale=vecs[:, col:col + 1])
                last.then_inc(acc_taken, 1)

            for j in range(NQ):
                q = Q_MIX + 2 * j

                def at(k):
                    if j == 0 and k == 3:
                        prod_take(2 * NQ - 1, q)
                    if j == 0 and k == 6:
                        hi_part("op_m", NQ, m_hi[:, KB - NB:KB, :], prod[:, :, :])
                    if j > 0 and k == 3:
                        if j == 1:
                            act.wait_ge(fam["op_m"][2], NQ)
                        post_take(RMS_MIX, j - 1, q, 0, acc[(j - 1) % 2], sq1, V_POST_MIX)
                hi_units(q, 0, 8, after=at)

            hi_units(Q_FF, 0, 4)
            post_take(RMS_MIX, NQ - 1, Q_FF, 0, acc[1], sq1, V_POST_MIX)
            root(RMS_MIX, std1[:, :], bank4[:, 0:T], 4 * EPS)
            for j in range(NQ):
                act.wait_ge(x1_ready, j + 1)
                if j >= 2:
                    act.wait_ge(sq_used, NQ * RMS_X1 + j - 1)
                f(sq1[:, j % 2], xT[:, NB * j:NB * j + NB, :], ACT.Square).then_inc(sq_ready, 1)
            root(RMS_X1, std2[:, :], bank5[:, 0:T], EPS)
            for j in range(NQ):
                hi_part("op_h", NQ + j + 1, h_hi[:, 4 * j:4 * j + 4, :], hf1[:, j % 2])

            def ff(j, k, q, lag):
                if lag and k == 3:
                    summed(q, 0)
                    f(uff[:, :, :], acc[1][:, :, :]).then_inc(acc_taken, 1)
                if lag and k == 6:
                    hi_part("op_ff", j, act_hi[:, ds(4 * (j - 1), 4), :], uff[:, :, :])
                if k == 11:
                    summed(q, 8)
                    if not lag:
                        act.wait_ge(x1_ready, NQ)
                    else:
                        act.wait_ge(fam["op_ff"][0], j)
                    f(tg[:, :, :], acc[0][:, :, :], ACT.Tanh, scale=0.5)
                    f(graw[:, :, :], acc[0][:, :, :]).then_inc(acc_taken, 1)

            def first_ff(k):
                k += 4
                ff(0, k, Q_FF, False)
                if k == 8:
                    act.wait_ge(pt_done, 1)
                    f(pf[:, :, :], pair[:, 0:2, :]).then_inc(fam["op_p"][0], 1)
                    hi_part("op_p", 1, p_hi[:, :, :], pf[:, :, :])
            hi_units(Q_FF, 4, 12, after=first_ff)
            with act.Fori(1, NFF) as j:
                hi_units(Q_FF + 4 * j, 0, 16, after=lambda k: ff(j, k, Q_FF + 4 * j, True))

            for t in range(2):
                for i in range(2):
                    j, q = 2 * t + i, Q_FO + t * (FO_UNITS // 2)

                    def at(k):
                        if j == 0 and k < 8:
                            ff(NFF, k, q, True)
                        if j > 0 and k == 3:
                            if j == 1:
                                act.wait_ge(fam["op_ff"][2], NFF)
                            post_take(RMS_F, j - 1, q, FO_UNITS * i, acc[1 - i], sq_f, V_POST_FFN)
                    hi_units(q, FO_UNITS * i, FO_UNITS, after=at)

            def ple_take(c):
                summed(Q_PP, c + 1)
                f(ple[:, NB * c:NB * c + NB, :], acc[c % 2][:, :, :], scale=0.5).then_inc(acc_taken, 1)

            def x2_hi(j):
                hi_part("op_x2", j + 1, h_hi[:, 4 * j:4 * j + 4, :], xT[:, 4 * j:4 * j + 4, :])

            hi_units(Q_PP, 0, 4)
            post_take(RMS_F, NQ - 1, Q_PP, 0, acc[1], sq_f, V_POST_FFN)
            root(RMS_F, std_f[:, :], bank4[:, 0:T], 4 * EPS)
            ple_take(0)
            ple_take(1)
            hi_units(Q_PG, 0, 2)
            x2_hi(0)
            ple_take(2)
            ple_take(3)
            hi_units(Q_PG, 2, 2)
            for j in range(1, NQ):
                x2_hi(j)

            def tgate_take(j, q):
                summed(q, 0)
                if j:
                    act.wait_ge(o_ready, j)
                f(tgate[:, :, :], acc[j % 2][:, :, :], ACT.Tanh, scale=0.5).then_inc(acc_taken, 1)

            def rows_take(j):
                act.wait_ge(ot_done, j + 1)
                f(o_rows[:, :, CW * j:CW * j + CW],
                  pair[:, :, :].rearrange("p (a b) t -> p a (b t)", a=2)).then_inc(rows_ready, 1)

            hi_units(Q_PG, 4, 4)
            for j in range(1, NQ):
                def at(k):
                    if k == 3:
                        tgate_take(j - 1, Q_PG + 2 * j)
                    if k == 7:
                        rows_take(j - 1)
                hi_units(Q_PG + 2 * j, 0, 8, after=at)
            tgate_take(NQ - 1, Q_PG + 2 * NQ)
            rows_take(NQ - 1)

        @block.vector
        def _(dve):
            v = nc.vector

            def lo_units(q, k0, n, after=None, cols=2 * CW):
                for k in range(k0, k0 + n):
                    dve.wait_ge(w_hi_done, 4 * q + k + 1)
                    raw, high, low = (t[:, k % RING, :, :].rearrange("p a n -> p (a n)")[:, 0:cols]
                                      for t in (w_raw, w_hi, w_lo))
                    v.tensor_tensor(low, raw, high.bitcast(F32), ALU.subtract).then_inc(w_lo_done, 1)
                    if after:
                        after(k - k0)

            def lo_part(name, n, o, i, high):
                dve.wait_ge(fam[name][1], n)
                v.tensor_tensor(o, i, high.bitcast(F32), ALU.subtract).then_inc(fam[name][2], 1)

            def inverse(stage, o, i):
                dve.wait_ge(std_ready, stage + 1)
                v.reciprocal(o, i).then_inc(rstd_ready, 1)
                dve.wait_ge(rstd_ready, stage + 1)

            def normed(n0, x_, hf, rstd, gain):
                def low(j):
                    q4 = slice(NB * j, NB * j + NB)
                    lo_part("op_h", n0 + j + 1, h_lo[:, q4, :], hf[:, j % 2], h_hi[:, q4, :])
                for j in range(NQ):
                    if j >= 2:
                        dve.wait_ge(fam["op_h"][2], n0 + j - 1)
                    for n in range(NB):
                        b = NB * j + n
                        last = v.scalar_tensor_tensor(hf[:, j % 2, n, :], x_[:, b, :], vecs[:, gain + b:gain + b + 1],
                                                      rstd, ALU.mult, ALU.mult)
                    last.then_inc(fam["op_h"][0], 1)
                    if j:
                        low(j - 1)
                low(NQ - 1)

            dve.wait_ge(consts, N_CONSTS)
            dve.wait_ge(vec_landed, 16 * 12)
            by_half = dsk_row[:, :].rearrange("p (b h) -> p b h", h=2)
            for half in range(2):
                rows = slice(HD * half, HD * half + HD)
                v.tensor_copy(skip[rows, :], by_half[rows, :, half])
            lo_units(Q_DT, 0, 4, cols=CW)
            inverse(RMS_X, rstd0[:, :], std0[:, :])
            dve.wait_ge(vecs_ready, 1)
            normed(0, xT0, hf0, rstd0[:, :], V_PRE_MIX)

            steps = Chain(dve, dt_steps)
            H = slice(0, NH)

            def softplus(k):
                if k == 3:
                    dve.wait_ge(unit_used, 4)
                    steps.step(v.tensor_scalar(dt_v[H, :], bank4[H, T:2 * T], head_col[H, 0:1], None, ALU.add))
                    steps.wait()
                    steps.step(v.scalar_tensor_tensor(dt_r[H, :], dt_v[H, :], -1.0, dt_v[H, :], ALU.mult, ALU.max))
                if k == 4:
                    dve.wait_ge(dt_exp, 2)
                    steps.step(v.tensor_scalar(dt_u[H, :], dt_e[H, :], 1.0, None, ALU.add))
                if k == 5:
                    dve.wait_ge(dt_log, 1)
                    steps.step(v.tensor_scalar(dt_r[H, :], dt_u[H, :], -1.0, None, ALU.add))
                    steps.wait()
                    steps.step(v.tensor_tensor(dt_e[H, :], dt_e[H, :], dt_r[H, :], ALU.subtract))
                    steps.wait()
                    steps.step(v.reciprocal(dt_r[H, :], dt_u[H, :]))
                    steps.wait()
                    steps.step(v.tensor_tensor(dt_e[H, :], dt_e[H, :], dt_r[H, :], ALU.mult))
                    steps.wait()
                    steps.step(v.tensor_tensor(dt_ln[H, :], dt_ln[H, :], dt_e[H, :], ALU.add))
                    steps.wait()
                    steps.step(v.scalar_tensor_tensor(dt_T[H, :], dt_v[H, :], 0.0, dt_ln[H, :], ALU.max, ALU.add))
                    steps.wait()
                    steps.step(v.tensor_scalar(dt_a[H, :], dt_T[H, :], head_col[H, 2:3], -1.0, ALU.mult, ALU.mult))
                    steps.wait()
                    for i in range(2):
                        c = slice(CH * i, CH * i + CH)
                        steps.step(v.tensor_tensor_scan(cum_T[H, c], ones[H, 0:CH], dt_a[H, c], 0.0, ALU.mult, ALU.add))
                    assert steps.n == DT_STEPS
                if k == 7:
                    dve.wait_ge(tok_done, 1)
                    v.tensor_copy(tok_dt[:, :, :], bank5[:, 0:2 * NH].rearrange("p (c h) -> p c h", h=NH))
                    v.tensor_copy(tok_cum[:, :, :],
                                  bank5[:, 2 * NH:4 * NH].rearrange("p (c h) -> p c h", h=NH)).then_inc(tok_ready, 1)

            lo_units(Q_BC, 0, 8, after=softplus)

            def conv_blocks(n, c, block0, pair_):
                if pair_ == 0:
                    dve.wait_ge(acc_taken, c + 1)
                chain = Chain(dve, conv_acc, CONV_STEPS * n + 8 * pair_)
                col = lambda tap, b: cwb[:, ds(NCB * tap + block0 + b, 1)]
                for t in range(TAPS):
                    for b in (2 * pair_, 2 * pair_ + 1):
                        if t == 0:
                            chain.step(v.tensor_scalar(xs[:, b, :], xraw[:, b, :], col(TAPS - 1, b), col(TAPS, b),
                                                       ALU.mult, ALU.add))
                        else:
                            chain.wait(chain.n - 1)
                            chain.step(v.scalar_tensor_tensor(xs[:, b, t:T], xraw[:, b, 0:T - t], col(TAPS - 1 - t, b),
                                                              xs[:, b, t:T], ALU.mult, ALU.add))
                assert chain.n == CONV_STEPS // 2

            def conv_end(n, o):
                dve.wait_ge(conv_tanh, n + 1)
                v.scalar_tensor_tensor(o, xraw[:, :, :], 1.0, xs[:, :, :], ALU.add, ALU.mult).then_inc(conv_out, 1)

            def conv_bc(n, k):
                if k == 3 or k == 4:
                    conv_blocks(n, C_BC + n, DI // P + NB * n, k - 3)
                if k == 7:
                    conv_end(n, bc[:, ds(NB * n, NB), :])

            with dve.Fori(1, 4) as c:
                lo_units(Q_BC + 2 * c, 0, 8, after=lambda k: conv_bc(c - 1, k))

            def scan_part(k, p_, z_chunk):
                heads = ds(HEADS * p_, HEADS)
                if k == 0:
                    dve.wait_ge(cb_done, p_ + 1)
                    v.tensor_tensor(cbm[:, :, :], bank4[:, 0:2 * CH].rearrange("p (c t) -> p c t", t=CH),
                                    mask[:, :].unsqueeze(1).to_broadcast([P, 2, CH]), ALU.mult).then_inc(cb_taken, 1)
                    dve.wait_ge(cum_landed, 48 * (p_ + 1))
                    v.tensor_tensor(to_end[:, :], decay[:, :, CH - 1], tok_cum[:, 0, heads],
                                    ALU.subtract).then_inc(end_ready, 1)
                    for i in (1, 0):
                        if i == 0:
                            dve.wait_ge(end_ready, p_ + 1)
                        for r in range(HEADS):
                            seg = decay[:, r, CH * i:CH * i + CH]
                            last = v.tensor_scalar(seg, seg, tok_cum[:, i, ds(HEADS * p_ + r, 1)], 0.0,
                                                   ALU.subtract, ALU.min)
                    last.then_inc(seg_ready, 1)
                if k == 2:
                    dve.wait_ge(decay_ready, p_ + 1)
                    dve.wait_ge(cb_taken, p_ + 1)
                    both = cbm[:, :, :].rearrange("p c t -> p (c t)").unsqueeze(1).to_broadcast([P, HEADS, T])
                    v.tensor_tensor(decay[:, :, :], decay[:, :, :], both, ALU.mult).then_inc(w_ready, 1)
                if k == 3:
                    dve.wait_ge(xtr_done, p_ + 1)
                    for i, bank in enumerate((bank4, bank5)):
                        v.tensor_tensor(xdt[:, i, :, :], bank[:, :].rearrange("p (h d) -> p h d", d=HD),
                                        tok_dt[:, i, heads].unsqueeze(2).to_broadcast([P, HEADS, HD]),
                                        ALU.mult).then_inc(xdt_ready, 1)
                    dve.wait_ge(xdt_ready, 2 * p_ + 1)
                    v.tensor_tensor(xend[:, :, :], xdt[:, 0, :, :], to_end[:, :].unsqueeze(2).to_broadcast([P, HEADS, HD]),
                                    ALU.mult).then_inc(xend_ready, 1)
                chain = Chain(dve, y_steps, Y_STEPS * p_)
                if k == 5:
                    dve.wait_ge(acc_taken, z_chunk + 1)
                    chain.step(v.scalar_tensor_tensor(zraw[:, :, :], ztanh[:, :, :], 1.0, zraw[:, :, :], ALU.add, ALU.mult))
                if k == 8:
                    chain.n = 1
                    chain.wait()
                    dve.wait_ge(y_done, p_ + 1)
                    for n in range(NB):
                        chain.step(v.scalar_tensor_tensor(yg[:, n, :], xs[:, n, :], skip[:, ds(NB * p_ + n, 1)],
                                                          pair[:, n, :], ALU.mult, ALU.add))
                    chain.step(v.tensor_tensor(ztanh[:, :, 0:CH], bank5[:, :].rearrange("p (b t) -> p b t", t=CH),
                                               ecum[:, :, :], ALU.mult))
                    chain.wait()
                    chain.step(v.tensor_tensor(yg[:, :, CH:T], yg[:, :, CH:T], ztanh[:, :, 0:CH], ALU.add))
                    assert chain.n == Y_STEPS
                if k == 9:
                    dve.wait_ge(y_steps, Y_STEPS * (p_ + 1))
                    v.tensor_tensor(yg[:, :, :], yg[:, :, :], zraw[:, :, :], ALU.mult).then_inc(y_gated, 1)
                if k == 10:
                    dve.wait_ge(ysq_ready, p_ + 1)
                    v.tensor_reduce(ysum[:, :], ztanh[:, :, :].rearrange("p b t -> p t b"), axis=AX.X,
                                    op=ALU.add).then_inc(ysum_ready, 1)
                if k == 12:
                    dve.wait_ge(ystd_ready, p_ + 1)
                    v.reciprocal(ystd[:, :], ystd[:, :]).then_inc(yrstd_ready, 1)
                if k == 14:
                    dve.wait_ge(yrstd_ready, p_ + 1)
                    for n in range(NB):
                        last = v.scalar_tensor_tensor(yg[:, n, :], yg[:, n, :], vecs[:, ds(V_SSM + NB * p_ + n, 1)],
                                                      ystd[:, :], ALU.mult, ALU.mult)
                    last.then_inc(fam["op_y"][0], 1)
                if k == 15:
                    four = ds(NB * p_, NB)
                    lo_part("op_y", p_ + 1, y_lo[:, four, :], yg[:, :, :], y_hi[:, four, :])

            def group(g, lag):
                def at(k):
                    if lag:
                        scan_part(k, g - 1, C_SSD + 2 * g - 1)
                    else:
                        conv_bc(3, k)
                    if k == 11 or k == 13:
                        conv_blocks(4 + g, C_SSD + 2 * g, NB * g, (k - 11) // 2)
                    if k == 15:
                        conv_end(4 + g, xs[:, :, :])
                lo_units(Q_SSD + 4 * g, 0, 16, after=at)

            dve.wait_ge(tok_ready, 1)
            group(0, False)
            with dve.Fori(1, GROUPS) as g:
                group(g, True)

            def windows(m, c):
                w = WINDOWS[m]
                chain = Chain(dve, pool_steps, POOL_STEPS * m + 1)
                dve.wait_ge(acc_taken, c + 1)
                chain.wait()
                if m:
                    dve.wait_ge(fam["op_pool"][2], m)
                for n in range(NB):
                    chain.step(v.tensor_tensor_scan(csum[:, n, 16:16 + T], ones[:, :], uraw[:, n, :], 0.0, ALU.mult, ALU.add))
                chain.wait()
                chain.step(v.tensor_tensor(ptmp[:, :, :], csum[:, :, 16:16 + T], csum[:, :, 16 - w:16 - w + T], ALU.subtract))
                chain.wait()
                chain.step(v.scalar_tensor_tensor(ptmp[:, :, 16:T], ptmp[:, :, 16:T], 1.0 / w, uraw[:, :, 16:T],
                                                  ALU.mult, ALU.subtract))
                chain.step(v.tensor_tensor(ptmp[:, :, 0:16], ptmp[:, :, 0:16],
                                           inv_n[:, m, :].unsqueeze(1).to_broadcast([P, NB, 16]), ALU.mult))
                chain.wait()
                v.tensor_tensor(ptmp[:, :, 0:16], ptmp[:, :, 0:16], uraw[:, :, 0:16],
                                ALU.subtract).then_inc(fam["op_pool"][0], 1)
                assert chain.n == POOL_STEPS

            def yp_low(m):
                q4 = slice(NB * m, NB * m + NB)
                lo_part("op_yp", m + 1, yp_lo[:, q4, :], uraw[:, :, :], yp_hi[:, q4, :])

            for h in range(2):
                c, q = C_POOL + 4 * h, Q_POOL + 5 * h

                def at(k):
                    if h == 0:
                        scan_part(k, GROUPS - 1, C_POOL - 1)
                    else:
                        if k == 2:
                            yp_low(0)
                        if k == 5:
                            yp_low(1)
                    if h == 0 and k == 11:
                        dve.wait_ge(ysum_ready, GROUPS)
                        v.memset(csum[:, :, 0:16], 0.0).then_inc(pool_steps, 1)
                    if k == 13:
                        windows(2 * h, c)
                lo_units(q, 0, 16, after=at)
                lo_part("op_pool", 2 * h + 1, pool_lo[:, 0], ptmp[:, :, :], pool_hi[:, 0])
                lo_units(q, 16, 4)
                windows(2 * h + 1, c + 1)
                lo_part("op_pool", 2 * h + 2, pool_lo[:, 1], ptmp[:, :, :], pool_hi[:, 1])

            def merge(m, j, own):
                dve.wait_ge(acc_taken, C_PO + 2 * m + 2)
                dst = prod[:, :, :] if own else mpool[:, ds(NB * j, NB), :]
                v.scalar_tensor_tensor(dst, gate[:, :, :], 1.0, prod[:, :, :], ALU.add, ALU.mult).then_inc(merged, 1)
                if own:
                    dve.wait_ge(merged, m + 1)
                    v.tensor_tensor(dst, dst, mpool[:, ds(NB * j, NB), :], ALU.add).then_inc(fam["op_m"][0], 1)

            def m_low(j):
                four = ds(NB * j, NB)
                lo_part("op_m", j + 1, m_lo[:, four, :], prod[:, :, :], m_hi[:, four, :])

            def po(j, q, first):
                def at(k):
                    if first and k == 2:
                        yp_low(2)
                    if first and k == 5:
                        yp_low(3)
                    if not first and k == 4:
                        merge(j - 1, j - 1, False)
                lo_units(q, 0, 16, after=at)

            po(0, Q_PO, True)
            with dve.Fori(1, NQ) as j:
                po(j, Q_PO + 4 * j, False)

            def so(j, q, first):
                def at(k):
                    if k == 4:
                        if first:
                            merge(NQ - 1, NQ - 1, False)
                        else:
                            merge(NQ + j - 1, j - 1, True)
                    if k == 6 and not first:
                        m_low(j - 1)
                lo_units(q, 0, 24, after=at)

            so(0, Q_SO, True)
            with dve.Fori(1, NQ) as j:
                so(j, Q_SO + 6 * j, False)

            def last_merge(k):
                if k == 4:
                    merge(2 * NQ - 1, NQ - 1, True)
                if k == 6:
                    m_low(NQ - 1)
            lo_units(Q_MIX, 0, 8, after=last_merge)
            with dve.Fori(1, NQ) as j:
                lo_units(Q_MIX + 2 * j, 0, 8)

            def residual(n, x_, rstd, ready):
                r = rstd.unsqueeze(1).to_broadcast([P, NB, T])

                def scaled(j):
                    four = fg[:, NB * j:NB * j + NB, :]
                    v.tensor_tensor(four, four, r, ALU.mult).then_inc(res_steps, 1)

                def added(j):
                    dve.wait_ge(res_steps, NQ * n + j + 1)
                    four = xT[:, NB * j:NB * j + NB, :]
                    v.tensor_tensor(four, x_[:, NB * j:NB * j + NB, :], fg[:, NB * j:NB * j + NB, :],
                                    ALU.add).then_inc(ready, 1)
                return scaled, added

            lo_units(Q_FF, 0, 4)
            inverse(RMS_MIX, rstd1[:, :], std1[:, :])
            dve.wait_ge(xT_landed, 16)
            scaled, added = residual(0, x_back, rstd1[:, :], x1_ready)
            scaled(0)
            for j in range(NQ):
                if j + 1 < NQ:
                    scaled(j + 1)
                added(j)
            inverse(RMS_X1, rstd2[:, :], std2[:, :])
            dve.wait_ge(x1_ready, NQ)
            normed(NQ, xT, hf1, rstd2[:, :], V_PRE_FFN)

            def ff(j, k, lag):
                if lag and k == 4:
                    dve.wait_ge(acc_taken, C_FF + 2 * j)
                    dve.wait_ge(gg_ready, j)
                    v.tensor_tensor(uff[:, :, :], uff[:, :, :], graw[:, :, :], ALU.mult).then_inc(fam["op_ff"][0], 1)
                if lag and k == 6:
                    four = ds(NB * (j - 1), NB)
                    lo_part("op_ff", j, act_lo[:, four, :], uff[:, :, :], act_hi[:, four, :])
                if k == 12:
                    dve.wait_ge(acc_taken, C_FF + 2 * j + 1)
                    v.scalar_tensor_tensor(graw[:, :, :], tg[:, :, :], 1.0, graw[:, :, :],
                                           ALU.add, ALU.mult).then_inc(gg_ready, 1)

            def first_ff(k):
                ff(0, k + 4, False)
                if k + 4 == 9:
                    lo_part("op_p", 1, p_lo[:, :, :], pf[:, :, :], p_hi[:, :, :])
            lo_units(Q_FF, 4, 12, after=first_ff)
            with dve.Fori(1, NFF) as j:
                lo_units(Q_FF + 4 * j, 0, 16, after=lambda k: ff(j, k, True))

            lo_units(Q_FO, 0, FO_UNITS, after=lambda k: k < 8 and ff(NFF, k, True))
            lo_units(Q_FO, FO_UNITS, FO_UNITS)
            lo_units(Q_FO + FO_UNITS // 2, 0, 2 * FO_UNITS)

            def x2_lo(j):
                four = slice(NB * j, NB * j + NB)
                lo_part("op_x2", j + 1, h_lo[:, four, :], xT[:, four, :], h_hi[:, four, :])

            lo_units(Q_PP, 0, 4)
            inverse(RMS_F, rstd_f[:, :], std_f[:, :])
            scaled, added = residual(1, xT, rstd_f[:, :], fam["op_x2"][0])
            scaled(0)
            scaled(1)
            added(0)
            added(1)
            lo_units(Q_PG, 0, 2)
            x2_lo(0)
            scaled(2)
            scaled(3)
            added(2)
            x2_lo(1)
            added(3)
            lo_units(Q_PG, 2, 2)
            x2_lo(2)
            x2_lo(3)

            def output(j):
                four = slice(NB * j, NB * j + NB)
                dve.wait_ge(acc_taken, C_PG + j + 1)
                if j:
                    dve.wait_ge(ot_done, j)
                v.scalar_tensor_tensor(o_T[:, :, :], tgate[:, :, :], 1.0, ple[:, four, :],
                                       ALU.add, ALU.mult).then_inc(o_steps, 1)
                dve.wait_ge(o_steps, j + 1)
                v.tensor_tensor(o_T[:, :, :], o_T[:, :, :], xT[:, four, :], ALU.add).then_inc(o_ready, 1)

            lo_units(Q_PG, 4, 4)
            for j in range(1, NQ):
                lo_units(Q_PG + 2 * j, 0, 8, after=lambda k: k == 3 and output(j - 1))
            output(NQ - 1)


_INS = ["x", "p", "w_in", "conv_w", "conv_b", "dt_bias", "a_log", "d_skip", "ssm_norm_g", "w_ssm_out",
        "w_pool_grp", "pool_scale", "w_pool_out", "w_mix_out", "g_pre_mix", "g_post_mix",
        "g_pre_ffn", "g_post_ffn", "w_ffn_in", "w_ffn_out", "w_ple_proj", "w_ple_gate"]


def kernel(**inputs):
    import numpy as _np
    import concourse.bacc as _bacc
    from concourse import mybir as _mybir
    from concourse.bass_utils import run_bass_kernel_spmd as _run

    nc = _bacc.Bacc("TRN2", target_bir_lowering=False, num_devices=1)
    arrays, args = {}, []
    for name in _INS:
        a = _np.ascontiguousarray(inputs[name])
        arrays[f"in_{name}_dram"] = a
        args.append(nc.dram_tensor(f"in_{name}_dram", a.shape, _mybir.dt.from_np(a.dtype), kind="ExternalInput").ap())
    args.append(nc.dram_tensor("out_dram", (1, T, D), F32, kind="ExternalOutput").ap())
    build(nc, *args)
    r = _run(nc, [arrays], core_ids=[0])
    return r.results[0]["out_dram"]
```

```python
from contextlib import ExitStack

import numpy as np

import concourse.bass as bass
from concourse import mybir
from concourse.bass import ds

F32 = mybir.dt.float32
F32R = mybir.dt.float32r
ACT = mybir.ActivationFunctionType
ALU = mybir.AluOpType
AX = mybir.AxisListType

P = 128
T = 256
D = 2048
DI = 4096
GROUPS, HEADS, HD = 8, 8, 64
NH = GROUPS * HEADS
CH = 128
CONV = DI + 2 * GROUPS * CH
TAPS = 4
FF = 5632
PLE = 256
EPS = 1e-6
WINDOWS = (2, 4, 8, 16)
CW = 512
NB = CW // P
KB = D // P
NQ = D // CW
Z0, XBC0, DT0 = 0, DI, DI + CONV
U0 = DT0 + NH
GS0, GP0 = U0 + D, U0 + 2 * D


RING = 4
Q_B0 = 0
Q_DT = Q_B0 + 2
Q_BC = Q_DT - 1
Q_SSD = Q_BC + 4 * 2
Q_POOL = Q_SSD + GROUPS * 4
Q_PO = Q_POOL + 10
Q_SO = Q_PO + NQ * 4
Q_MIX = Q_SO + NQ * 6
Q_FF = Q_MIX + NQ * 2
NFF = FF // CW
Q_FO = Q_FF + NFF * 4
FO_UNITS = FF // (2 * P)
Q_PP = Q_FO + NQ * FO_UNITS // 4
Q_PG = Q_PP + 1

C_BC = 0
C_SSD = C_BC + 4
C_POOL = C_SSD + 2 * GROUPS
C_PO = C_POOL + 8
C_SO = C_PO + 2 * NQ
C_MIX = C_SO + 2 * NQ
C_FF = C_MIX + NQ
C_FO = C_FF + 2 * NFF
C_PP = C_FO + NQ
C_PG = C_PP + NQ

V_PRE_MIX, V_POST_MIX, V_PRE_FFN, V_POST_FFN, V_POOL, V_SSM = 0, KB, 2 * KB, 3 * KB, 4 * KB, 5 * KB
N_VECS = 5 * KB + DI // P
NCB = CONV // P

RMS_X, RMS_MIX, RMS_X1, RMS_F = range(4)
SQ_ADDED = {RMS_X: 0, RMS_MIX: 2, RMS_F: 4}
SQ_DONE = {RMS_X: 2, RMS_MIX: 4, RMS_X1: 8, RMS_F: 10}
PIECES = KB // 2
DT_STEPS = 12
CONV_STEPS = NB * TAPS
Y_STEPS = NB + 3
POOL_STEPS = NB + 4


def windows_of(sums, m):
    return sums[:, :, 16 - WINDOWS[m]:16 - WINDOWS[m] + T]


class Chain:

    def __init__(self, engine, sem, done=0):
        self.engine, self.sem, self.start, self.n = engine, sem, done, 0

    def step(self, instruction):
        instruction.then_inc(self.sem, 1)
        self.n += 1
        return self.n

    def wait(self, n=None):
        self.engine.wait_ge(self.sem, self.start + (self.n if n is None else n))


def build(nc, x, p, w_in, conv_w, conv_b, dt_bias, a_log, d_skip, ssm_norm_g, w_ssm_out,
          w_pool_grp, pool_scale, w_pool_out, w_mix_out, g_pre_mix, g_post_mix,
          g_pre_ffn, g_post_ffn, w_ffn_in, w_ffn_out, w_ple_proj, w_ple_gate, out):
    w_in, w_ssm_out, w_pool_out, w_mix_out = w_in[0], w_ssm_out[0], w_pool_out[0], w_mix_out[0]
    w_ffn_in, w_ffn_out, w_ple_proj, w_ple_gate = w_ffn_in[0], w_ffn_out[0], w_ple_proj[0], w_ple_gate[0]
    x_rows = x[0].rearrange("(a p) n -> p a n", p=P)
    p_rows = p[0, 0].rearrange("(a p) n -> p a n", p=P)
    out_rows = out[0].rearrange("(a p) n -> p a n", p=P)
    cum_dram = nc.dram_tensor("cum_scratch", (NH, T), F32, kind="Internal").ap()
    xT_dram = nc.dram_tensor("xT_scratch", (P, KB, T), F32, kind="Internal").ap()

    SBUF0 = (nc.sbuf_base + 63) // 64 * 64
    def place(name, shape, dt, kb):
        return nc.alloc_sbuf_tensor_at(name, [P] + shape, dt, offset=SBUF0 + int(kb * 1024)).ap()

    h_hi, h_lo = place("h_hi", [KB, T], F32R, 0), place("h_lo", [KB, T], F32R, 16)
    y_hi, y_lo = place("y_hi", [2 * KB, T], F32R, 32), place("y_lo", [2 * KB, T], F32R, 64)
    x_in = place("x_in", [2, D], F32, 32)
    xT0 = place("xT0", [KB, T], F32, 48)
    sq0 = place("sq0", [2, NB, T], F32, 64)
    hf0 = place("hf0", [4, 2, T], F32, 72)
    sqs0 = place("sqs0", [NB, T], F32, 28)
    vrow = place("vrow", [4, P], F32, 80)
    dsk_row = place("dsk_row", [NH], F32, 82)
    head_col = place("head_col", [4], F32, 82.5)
    rstd0 = place("rstd0", [T], F32, 84)
    dt_v, dt_e, dt_u, dt_ln = (place(n, [T], F32, kb) for n, kb in
                               (("dt_v", 85), ("dt_e", 86), ("dt_u", 87), ("dt_ln", 88)))
    dt_r, dt_T, dt_a, cum_T = (place(n, [T], F32, kb) for n, kb in
                               (("dt_r", 89), ("dt_T", 90), ("dt_a", 91), ("cum_T", 92)))
    bc = place("bc", [2 * GROUPS, T], F32, 96)
    decay = place("decay", [HEADS, T], F32, 112)
    xraw = place("xraw", [NB, T], F32, 120)
    xs = place("xs", [NB, T], F32, 124)
    zraw = place("zraw", [NB, T], F32, 128)
    ztanh = place("ztanh", [NB, T], F32, 132)
    xdt = place("xdt", [2, HEADS, HD], F32, 136)
    xend = place("xend", [HEADS, HD], F32, 140)
    state = place("state", [HEADS * HD], F32, 142)
    yg = place("yg", [NB, T], F32, 144)
    ecum = place("ecum", [NB, CH], F32, 148)
    bn = place("bn", [CH], F32, 150)
    cbm = place("cbm", [2, CH], F32, 150.5)
    ysum = place("ysum", [T], F32, 151.5)
    yrstd = place("yrstd", [T], F32, 152.5)
    mask = place("mask", [CH], F32, 153.5)
    cwb = place("cwb", [(TAPS + 1) * NCB], F32, 154)
    tok_dt = place("tok_dt", [2, NH], F32, 155)
    tok_cum = place("tok_cum", [2, NH], F32, 155.5)
    skip = place("skip", [DI // P], F32, 156)
    to_end = place("to_end", [HEADS], F32, 156.25)
    b_own = place("b_own", [T], F32, 156.5)
    yp_hi, yp_lo = place("yp_hi", [KB, T], F32R, 96), place("yp_lo", [KB, T], F32R, 112)
    uraw = place("uraw", [NB, T], F32, 128)
    csum = place("csum", [NB, 16 + T], F32, 132)
    ypf = place("ypf", [NB, T], F32, 136.25)
    pool_hi = [place(f"pool_hi{m}", [NB, T], F32R, kb) for m, kb in enumerate((104, 108, 140.25, 144.25))]
    pool_lo = [place(f"pool_lo{m}", [NB, T], F32R, kb) for m, kb in enumerate((120, 124, 148.25, 152.25))]
    mpool = place("mpool", [KB, T], F32, 128)
    gate = place("gate", [NB, T], F32, 144)
    prod = place("prod", [NB, T], F32, 148)
    m_hi, m_lo = place("m_hi", [KB, T], F32R, 96), place("m_lo", [KB, T], F32R, 112)
    act_hi, act_lo = place("act_hi", [FF // P, T], F32R, 32), place("act_lo", [FF // P, T], F32R, 76)
    x_back = place("x_back", [KB, T], F32, 52)
    xT = place("xT", [KB, T], F32, 120)
    fg = place("fg", [KB, T], F32, 136)
    sq1 = place("sq1", [2, NB, T], F32, 32)
    hf1 = place("hf1", [4, 2, T], F32, 40)
    sqs1 = place("sqs1", [NB, T], F32, 76)
    rstd1 = place("rstd1", [T], F32, 48)
    rstd2 = place("rstd2", [T], F32, 148)
    p_in = place("p_in", [2, PLE], F32, 72)
    pf = place("pf", [2, T], F32, 74)
    p_hi, p_lo = place("p_hi", [2, T], F32R, 152), place("p_lo", [2, T], F32R, 154)
    tg = place("tg", [NB, T], F32, 136)
    graw = place("graw", [NB, T], F32, 140)
    uff = place("uff", [NB, T], F32, 144)
    sq_f = place("sq_f", [2, NB, T], F32, 0)
    sqs_f = place("sqs_f", [NB, T], F32, 8)
    ple = place("ple", [KB, T], F32, 32)
    rstd_f = place("rstd_f", [T], F32, 48)
    tgate = place("tgate", [NB, T], F32, 52)
    o_T = place("o_T", [NB, T], F32, 56)
    o_rows = place("o_rows", [2, D], F32, 60)
    ident = place("ident", [P], F32, 157.5)
    mean_w = place("mean_w", [P], F32, 158)
    ones = place("ones", [P], F32, 158.5)
    vecs = place("vecs", [N_VECS], F32, 159)
    inv_n = place("inv_n", [len(WINDOWS), 16], F32, 159.5)
    RING0 = 159.84375
    w_raw = place("w_raw", [RING, 2, CW], F32, RING0)
    w_hi = place("w_hi", [RING, 2, CW], F32R, RING0 + 16)
    w_lo = place("w_lo", [RING, 2, CW], F32R, RING0 + 32)

    ctx = ExitStack()
    with ctx:
        acc = [ctx.enter_context(nc.psum_tensor(f"acc{i}", [P, NB, T], F32)) for i in range(2)]
        bank4 = ctx.enter_context(nc.psum_tensor("bank4", [P, 512], F32))
        bank5 = ctx.enter_context(nc.psum_tensor("bank5", [P, 512], F32))
        pair = ctx.enter_context(nc.psum_tensor("pair", [P, NB, T], F32))

        def sem(name):
            return ctx.enter_context(nc.semaphore(name))

        w_landed = [sem(f"w_landed{i}") for i in range(RING)]
        w_hi_done, w_lo_done = sem("w_hi_done"), sem("w_lo_done")
        unit_used = sem("unit_used")
        half_done = sem("half_done")
        acc_taken = sem("acc_taken")
        x_landed = [sem(f"x_landed{i}") for i in range(NQ)]
        vec_landed, consts = sem("vec_landed"), sem("consts")
        vecs_t, vecs_ready = sem("vecs_t"), sem("vecs_ready")
        xt_done, xT_stored = sem("xt_done"), sem("xT_stored")
        sq_ready, sq_added, sq_used = sem("sq_ready"), sem("sq_added"), sem("sq_used")
        sq_half, std_ready, rstd_ready = sem("sq_half"), sem("std_ready"), sem("rstd_ready")
        fam = {n: (sem(n + "_f"), sem(n + "_h"), sem(n + "_l"))
               for n in ("op_h", "op_y", "op_pool", "op_yp", "op_m", "op_ff", "op_x2", "op_p")}
        dt_steps, dt_exp, dt_log = sem("dt_steps"), sem("dt_exp"), sem("dt_log")
        tok_done, tok_ready, cum_stored, cum_landed = (sem("tok_done"), sem("tok_ready"),
                                                       sem("cum_stored"), sem("cum_landed"))
        conv_acc, conv_tanh, conv_out = sem("conv_acc"), sem("conv_tanh"), sem("conv_out")
        cb_done, cb_taken, bn_taken, b_ready = sem("cb_done"), sem("cb_taken"), sem("bn_taken"), sem("b_ready")
        fall_ready = sem("fall_ready")
        end_ready, decay_ready, w_ready = sem("end_ready"), sem("decay_ready"), sem("w_ready")
        xtr_done, xdt_ready, xend_ready = sem("xtr_done"), sem("xdt_ready"), sem("xend_ready")
        state_done, state_ready, y_done = sem("state_done"), sem("state_ready"), sem("y_done")
        y_steps, y_gated, ysq_ready, ysum_ready = sem("y_steps"), sem("y_gated"), sem("ysq_ready"), sem("ysum_ready")
        yss_done, ystd_ready, yrstd_ready = sem("yss_done"), sem("ystd_ready"), sem("yrstd_ready")
        pool_steps, merged = sem("pool_steps"), sem("merged")
        xT_landed, res_steps = sem("xT_landed"), sem("res_steps")
        x1_ready = sem("x1_ready")
        p_landed, pt_done = sem("p_landed"), sem("pt_done")
        gtanh_ready, gg_ready = sem("gtanh_ready"), sem("gg_ready")
        last_gate, rows_late = sem("last_gate"), sem("rows_late")
        o_steps, o_ready = sem("o_steps"), sem("o_ready")
        ot_done, rows_ready, out_stored = sem("ot_done"), sem("rows_ready"), sem("out_stored")

        block = ctx.enter_context(nc.Block())

        @block.sync
        def _(sp):
            def unit(q, k, src, cols=CW):
                u = 4 * q + k
                if not (isinstance(u, int) and u < RING):
                    sp.wait_ge(w_lo_done, u - RING + 1)
                dst = w_raw[:, k % RING, :, :].rearrange("p a n -> p (a n)")[:, 0:src.shape[1] * cols]
                sp.dma_start(dst.rearrange("p (k n) -> p k n", n=cols), src).then_inc(w_landed[k % RING], 16)

            def chunk(q, k0, w, col, blocks, row0=0, after=None):
                for k in range(blocks // 2):
                    r = row0 + 2 * P * k
                    unit(q, k0 + k, w[r:r + 2 * P, ds(col, CW)].rearrange("(k p) n -> p k n", p=P))
                    if after:
                        after(k)

            for j in range(NQ):
                sp.dma_start(x_in[:, :, ds(CW * j, CW)], x_rows[:, :, ds(CW * j, CW)]).then_inc(x_landed[j], 16)
            at = 0
            for v in (g_pre_mix, g_post_mix, g_pre_ffn, g_post_ffn, pool_scale, ssm_norm_g):
                n = v.shape[1] // P
                sp.dma_start(vrow[at:at + n, 0, :], v[0].rearrange("(b c) -> b c", c=P)).then_inc(vec_landed, 16)
                at += n
            taps = conv_w[0].rearrange("k (b c) -> (k b) c", c=P)
            for i in range(2):
                sp.dma_start(vrow[0:96, 1 + i, :], taps[96 * i:96 * i + 96, :]).then_inc(vec_landed, 16)
            sp.dma_start(vrow[0:NCB, 3, :], conv_b[0].rearrange("(b c) -> b c", c=P)).then_inc(vec_landed, 16)
            sp.dma_start(head_col[0:NH, 0:1], dt_bias[0].rearrange("(h a) -> h a", a=1)).then_inc(vec_landed, 16)
            sp.dma_start(head_col[0:NH, 1:2], a_log[0].rearrange("(h a) -> h a", a=1)).then_inc(vec_landed, 16)
            sp.dma_start(dsk_row[:, :], d_skip.to_broadcast([P, NH])).then_inc(vec_landed, 16)
            chunk(Q_B0, 0, w_in, XBC0 + DI, KB)
            for k in range(4):
                unit(Q_DT, k, w_in[CW * k:CW * k + CW, DT0:DT0 + P].rearrange("(k p) n -> p k n", p=P), P)

            with sp.Fori(1, 4) as c:
                chunk(Q_BC + 2 * c, 0, w_in, XBC0 + DI + CW * c, KB)

            def group(up, first):
                g, q = up - 1, Q_SSD - 4 + 4 * up
                chunk(q, 0, w_in, XBC0 - CW + CW * up, KB)

                def decays(k):
                    if k == 6:
                        if first:
                            sp.wait_ge(cum_stored, 16)
                        else:
                            sp.wait_ge(y_done, g)
                            sp.wait_ge(y_gated, g)
                        rows = cum_dram[ds(HEADS * g, HEADS), :]
                        everywhere = rows.unsqueeze(0).to_broadcast([P, HEADS, T])
                        sp.dma_start(decay[:, :, :], everywhere).then_inc(cum_landed, 16)
                        for half in range(2):
                            odd = rows.rearrange("(b h) t -> h b t", h=2)[half:half + 1, :, CH:T]
                            sp.dma_start(ecum[HD * half:HD * half + HD, :, :],
                                         odd.to_broadcast([HD, NB, CH])).then_inc(cum_landed, 16)
                chunk(q, 8, w_in, CW * up + (Z0 - CW), KB, after=decays)

            group(1, True)
            with sp.Fori(2, GROUPS + 1) as up:
                group(up, False)

            for m in range(4):
                chunk(Q_POOL, 8 * m, w_in, U0 + CW * m, KB)
            for m in range(4):
                chunk(Q_POOL, 32 + 2 * m, w_pool_grp[0, m], 0, NB)

            def gated(q, gate_col, w, up, blocks):
                chunk(q, 0, w_in, gate_col - CW + CW * up, KB)
                chunk(q, 8, w, CW * up - CW, blocks)

            with sp.Fori(1, NQ + 1) as up:
                gated(Q_PO - 4 + 4 * up, GP0, w_pool_out, up, KB)
            with sp.Fori(1, NQ + 1) as up:
                gated(Q_SO - 6 + 6 * up, GS0, w_ssm_out, up, 2 * KB)
            with sp.Fori(0, NQ) as j:
                chunk(Q_MIX + 2 * j, 0, w_mix_out, CW * j, KB)
            sp.wait_ge(unit_used, 4 * Q_MIX)
            sp.wait_ge(xT_stored, 16)
            sp.dma_start(x_back[:, :, :], xT_dram).then_inc(xT_landed, 16)
            sp.dma_start(p_in[:, :, :], p_rows).then_inc(p_landed, 16)
            with sp.Fori(0, NFF) as j:
                chunk(Q_FF + 4 * j, 0, w_ffn_in, CW * j, KB)
                chunk(Q_FF + 4 * j, 8, w_ffn_in, FF + CW * j, KB)
            with sp.Fori(0, 2) as t:
                for i in range(2):
                    chunk(Q_FO + t * (FO_UNITS // 2), FO_UNITS * i, w_ffn_out, CW * (2 * t + i), FF // P)
            for c in range(NQ):
                chunk(Q_PP, c, w_ple_proj, CW * c, 2)
            with sp.Fori(0, NQ) as j:
                chunk(Q_PG + 2 * j, 0, w_ple_gate, CW * j, KB)
            late = D - CW // 2
            for n, (c0, c1, ready, count) in enumerate(((0, CW, rows_ready, 1), (CW, 2 * CW, rows_ready, 2),
                                                        (2 * CW, 3 * CW, rows_ready, 3), (3 * CW, late, rows_ready, 4),
                                                        (late, D, rows_late, 1))):
                sp.wait_ge(ready, count)
                sp.dma_start(out_rows[:, :, c0:c1], o_rows[:, :, c0:c1]).then_inc(out_stored, 16)
            sp.wait_ge(out_stored, 16 * (NQ + 1))

        @block.gpsimd
        def _(pool):
            pool.memset(ident[:, :], 0.0).then_inc(consts, 1)
            pool.memset(ones[:, :], 1.0).then_inc(consts, 1)
            pool.memset(mean_w[:, :], 1.0 / D).then_inc(consts, 1)
            pool.memset(mask[:, :], 1.0).then_inc(consts, 1)
            for i, w in enumerate(WINDOWS):
                pool.memset(inv_n[:, i, w - 1:16], 1.0 / w).then_inc(consts, 1)
                for t in range(w - 1):
                    pool.memset(inv_n[:, i, t:t + 1], 1.0 / (t + 1)).then_inc(consts, 1)
            n = 4 + sum(WINDOWS)
            pool.wait_ge(consts, n)
            pool.affine_select(out=ident[:, :], in_=ident[:, :], compare_op=ALU.not_equal, fill=1.0, base=0,
                               pattern=[[-1, P]], channel_multiplier=1).then_inc(consts, 1)
            pool.affine_select(out=mask[:, :], in_=mask[:, :], compare_op=ALU.is_ge, fill=0.0, base=0,
                               pattern=[[1, CH]], channel_multiplier=-1).then_inc(consts, 1)

        N_CONSTS = 4 + sum(WINDOWS) + 2

        @block.tensor
        def _(pe):
            def mm(o, l, r, first, last=True):
                return nc.tensor.matmul(o, lhsT=l, rhs=r, start=first, stop=last, skip_group_check=True)

            def turn(o, i, rows=P):
                return nc.tensor.transpose(o, i, ident[0:rows, 0:rows])

            def unit_products(q, k0, k, blocks, hi, lo, accum, columns):
                s = (k0 + k) % RING
                for a in range(2):
                    b = 2 * k + a
                    for n in columns:
                        o = accum[:, n, :]
                        wh = w_hi[:, s, a, P * n:P * n + P]
                        wl = w_lo[:, s, a, P * n:P * n + P]
                        mm(o, wh, hi[:, b, :], b == 0 and n % 2 == 0, False)
                        mm(o, wh, lo[:, b, :], False, False)
                        last = mm(o, wl, hi[:, b, :], False, b == blocks - 1)
                return last

            def product(c, q, k0, blocks, hi, lo, accum, wait_for=None, after=None, halves=False):
                if not (isinstance(c, int) and c < 2):
                    pe.wait_ge(acc_taken, c - 1)
                units = blocks // 2
                for k in range(units):
                    if wait_for:
                        wait_for(k)
                    if not halves or k < units - RING:
                        pe.wait_ge(w_lo_done, 4 * q + k0 + k + 1)
                    elif k == units - RING:
                        for late in range(k, units):
                            pe.wait_ge(w_lo_done, 4 * q + k0 + late + 1)
                            last = unit_products(q, k0, late, blocks, hi, lo, accum, (0, 1))
                        last.then_inc(half_done, 1)
                    columns = (2, 3) if halves and k >= units - RING else range(NB)
                    unit_products(q, k0, k, blocks, hi, lo, accum, columns).then_inc(unit_used, 1)
                    if after:
                        after(k)

            def means(o, squares, first, last):
                for n in range(NB):
                    done = mm(o, mean_w[:, :], squares[:, n, :], first and n == 0, last and n == NB - 1)
                done.then_inc(sq_used, 1)

            def three_quarters(stage, squares):
                pe.wait_ge(sq_added, SQ_ADDED[stage] + 2)
                means(ss, squares, True, False)

            def last_quarter(stage, squares):
                pe.wait_ge(sq_ready, NQ * stage + NQ)
                means(ss, squares, False, True)

            pe.wait_ge(consts, N_CONSTS)
            ss = bank4[:, 0:T]
            for j in range(NQ):
                pe.wait_ge(x_landed[j], 16)
                if j >= 2:
                    pe.wait_ge(sq_ready, j - 1)
                for n in range(NB):
                    for a in range(2):
                        last = turn(acc[j % 2][:, n, P * a:P * a + P], x_in[:, a, CW * j + P * n:CW * j + P * n + P])
                last.then_inc(xt_done, 1)
                if j == 2:
                    pe.wait_ge(vec_landed, 16 * 12)
                    turn(bank5[:, 0:N_VECS], vrow[0:N_VECS, 0, :], N_VECS)
                    turn(bank5[:, N_VECS:N_VECS + 96], vrow[0:96, 1, :], 96)
                    turn(bank5[:, N_VECS + 96:N_VECS + 192], vrow[0:96, 2, :], 96)
                    turn(bank5[:, N_VECS + 192:N_VECS + 240], vrow[0:NCB, 3, :], NCB).then_inc(vecs_t, 1)
            three_quarters(RMS_X, sqs0)
            last_quarter(RMS_X, sq0[:, 1])

            def by_token(k):
                if k == 1:
                    pe.wait_ge(dt_steps, DT_STEPS)
                    for i, t in enumerate((dt_T, cum_T)):
                        for a in range(2):
                            last = turn(bank5[:, P * i + NH * a:P * i + NH * a + NH],
                                        t[0:NH, P * a:P * a + P], NH)
                    last.then_inc(tok_done, 1)

            product(C_BC, Q_B0, 0, KB, h_hi, h_lo, acc[0],
                    wait_for=lambda k: pe.wait_ge(fam["op_h"][2], k + 1))
            dt_raw = bank4[:, T:2 * T]
            for k in range(4):
                pe.wait_ge(w_lo_done, 4 * Q_DT + k + 1)
                wh = w_hi[:, k, :, :].rearrange("p a n -> p (a n)")
                wl = w_lo[:, k, :, :].rearrange("p a n -> p (a n)")
                for a in range(4):
                    b, c = 4 * k + a, P * a
                    mm(dt_raw, wh[:, c:c + P], h_hi[:, b, :], b == 0, False)
                    mm(dt_raw, wh[:, c:c + P], h_lo[:, b, :], False, False)
                    last = mm(dt_raw, wl[:, c:c + P], h_hi[:, b, :], False, b == KB - 1)
                last.then_inc(unit_used, 1)
            product(C_BC + 1, Q_BC + 2, 0, KB, h_hi, h_lo, acc[1])
            product(C_BC + 2, Q_BC + 4, 0, KB, h_hi, h_lo, acc[0], after=by_token)
            product(C_BC + 3, Q_BC + 6, 0, KB, h_hi, h_lo, acc[1])

            def scan_turns(p_):
                pe.wait_ge(conv_out, 5 + p_)
                pe.wait_ge(cb_taken, p_ + 1)
                pe.wait_ge(bn_taken, p_ + 1)
                for i, bank in enumerate((bank4, bank5)):
                    for n in range(NB):
                        last = turn(bank[:, P * n:P * n + P], xs[:, n, CH * i:CH * i + CH])
                last.then_inc(xtr_done, 1)

            def intra(p_, i):
                for r in range(HEADS):
                    half, n = r % 2, r // 2
                    last = mm(pair[HD * half:HD * half + HD, n, CH * i:CH * i + CH],
                              xdt[:, i, r, :], decay[:, r, CH * i:CH * i + CH], True)
                return last

            def scan_first(p_):
                pe.wait_ge(xdt_ready, 2 * p_ + 2)
                pe.wait_ge(w_ready, p_ + 1)
                intra(p_, 0)
                pe.wait_ge(xend_ready, p_ + 1)
                mm(bank4[:, :], bn[:, :], xend[:, :, :].rearrange("p h d -> p (h d)"), True).then_inc(state_done, 1)

            def scan_second(p_):
                intra(p_, 1)
                pe.wait_ge(state_ready, p_ + 1)
                for n in range(NB):
                    last = mm(bank5[:, CH * n:CH * n + CH], state[:, P * n:P * n + P],
                              bc[:, ds(GROUPS + p_, 1), CH:T].rearrange("p a t -> p (a t)"), True)
                last.then_inc(y_done, 1)

            def y_squares(p_):
                pe.wait_ge(ysum_ready, p_ + 1)
                mm(pair[:, 0, :], mean_w[:, :], ysum[:, :], True).then_inc(yss_done, 1)

            def bc_products(g, first):
                pe.wait_ge(b_ready, g + 1)
                if not first:
                    pe.wait_ge(state_ready, g)
                    pe.wait_ge(y_gated, g)
                for i in range(2):
                    tokens = slice(CH * i, CH * i + CH)
                    mm(bank4[:, tokens], b_own[:, tokens],
                       bc[:, ds(GROUPS + g, 1), tokens].rearrange("p a t -> p (a t)"), True)
                turn(bank5[:, 0:CH], b_own[:, 0:CH]).then_inc(cb_done, 1)

            def group(g, c, q, own, lag):
                p_ = g - 1

                def a_side(k):
                    if lag:
                        if k == 0:
                            scan_turns(p_)
                        if k == 3:
                            scan_first(p_)
                        if k == 4:
                            scan_second(p_)

                def b_side(k):
                    if lag and k == 2:
                        y_squares(p_)
                    if own and k == 4:
                        bc_products(g, not lag)

                product(c, q, 0, KB, h_hi, h_lo, acc[0], after=a_side)
                product(c + 1, q, 8, KB, h_hi, h_lo, acc[1], after=b_side)

            group(0, C_SSD, Q_SSD, True, False)
            with pe.Fori(1, GROUPS) as g:
                group(g, C_SSD + 2 * g, Q_SSD + 4 * g, True, True)

            group(GROUPS, C_POOL, Q_POOL, False, True)
            group(GROUPS, C_POOL + 2, Q_POOL + 4, False, False)
            for m in range(4):
                product(C_POOL + 4 + m, Q_POOL, 32 + 2 * m, NB, pool_hi[m], pool_lo[m], acc[m % 2],
                        wait_for=lambda k: pe.wait_ge(fam["op_pool"][2], m + 1))

            def yp_quarter(k):
                pe.wait_ge(fam["op_yp"][2], k // 2 + 1)

            with pe.Fori(0, NQ) as j:
                product(C_PO + 2 * j, Q_PO + 4 * j, 0, KB, h_hi, h_lo, acc[0])
                product(C_PO + 1 + 2 * j, Q_PO + 4 * j, 8, KB, yp_hi, yp_lo, acc[1],
                        wait_for=lambda k: k % 2 == 0 and yp_quarter(k))
            pe.wait_ge(fam["op_y"][2], GROUPS)
            with pe.Fori(0, NQ) as j:
                product(C_SO + 2 * j, Q_SO + 6 * j, 0, KB, h_hi, h_lo, acc[0])
                product(C_SO + 1 + 2 * j, Q_SO + 6 * j, 8, 2 * KB, y_hi, y_lo, acc[1])
            for j in range(NQ):
                product(C_MIX + j, Q_MIX + 2 * j, 0, KB, m_hi, m_lo, acc[j % 2],
                        wait_for=lambda k: j == 0 and k % 2 == 0 and pe.wait_ge(fam["op_m"][2], k // 2 + 1),
                        after=lambda k: j == NQ - 1 and k == 5 and three_quarters(RMS_MIX, sqs1),
                        halves=j == NQ - 1)
            for half, ready, count in ((0, sq_half, 1), (1, sq_ready, NQ * RMS_MIX + NQ)):
                pe.wait_ge(ready, count)
                for n in (2 * half, 2 * half + 1):
                    last = mm(ss, mean_w[:, :], sq1[:, (NQ - 1) % 2, n, :], False, n == NB - 1)
            last.then_inc(sq_used, 1)

            def x1_squares(k):
                if k in (2, 4, 6, 7):
                    j = (k - 1) // 2
                    pe.wait_ge(sq_ready, NQ * RMS_X1 + j + 1)
                    means(bank5[:, 0:T], sq1[:, j % 2], j == 0, j == NQ - 1)
                if k == 7:
                    pe.wait_ge(p_landed, 16)
                    for n in range(2):
                        for a in range(2):
                            last = turn(pair[:, n, P * a:P * a + P], p_in[:, a, P * n:P * n + P])
                    last.then_inc(pt_done, 1)

            product(C_FF, Q_FF, 0, KB, h_hi, h_lo, acc[0], after=x1_squares,
                    wait_for=lambda k: pe.wait_ge(fam["op_h"][2], PIECES + k + 1))
            product(C_FF + 1, Q_FF, 8, KB, h_hi, h_lo, acc[1])
            with pe.Fori(1, NFF) as j:
                product(C_FF + 2 * j, Q_FF + 4 * j, 0, KB, h_hi, h_lo, acc[0])
                product(C_FF + 1 + 2 * j, Q_FF + 4 * j, 8, KB, h_hi, h_lo, acc[1])
            for t in range(2):
                for i in range(2):
                    j = 2 * t + i
                    product(C_FO + j, Q_FO + t * (FO_UNITS // 2), FO_UNITS * i, FF // P, act_hi, act_lo, acc[i],
                            wait_for=lambda k: j == 0 and k % 2 == 0 and pe.wait_ge(fam["op_ff"][2], k // 2 + 1),
                            after=lambda k: j == NQ - 1 and k == 8 and three_quarters(RMS_F, sqs_f))
            last_quarter(RMS_F, sq_f[:, 1])
            pe.wait_ge(fam["op_p"][2], 1)
            for c in range(NQ):
                product(C_PP + c, Q_PP, c, 2, p_hi, p_lo, acc[c % 2])

            def rows_out(j):
                pe.wait_ge(o_ready, j + 1)
                if not (isinstance(j, int) and j == 0):
                    pe.wait_ge(rows_ready, j)
                for a in range(2):
                    for n in range(NB):
                        last = turn(pair[:, 2 * a:2 * a + 2, :].rearrange("p b t -> p (b t)")[:, P * n:P * n + P],
                                    o_T[:, n, P * a:P * a + P])
                last.then_inc(ot_done, 1)

            for j in range(NQ):
                product(C_PG + j, Q_PG + 2 * j, 0, KB, h_hi, h_lo, acc[j % 2],
                        wait_for=lambda k: j == 0 and pe.wait_ge(fam["op_x2"][2], k + 1),
                        after=lambda k: j > 0 and k == 3 and rows_out(j - 1), halves=j == NQ - 1)
            for half in range(2):
                pe.wait_ge(o_ready, NQ + half)
                pe.wait_ge(rows_ready, NQ - 1)
                for a in range(2):
                    for n in range(2):
                        last = turn(pair[:, 2 * half + a, P * n:P * n + P], o_T[:, 2 * half + n, P * a:P * a + P])
                last.then_inc(ot_done, 1)

        @block.scalar
        def _(act):
            def f(o, i, fn=ACT.Copy, **kw):
                return nc.scalar.activation(o, i, fn, **kw)

            def hi_units(q, k0, n, after=None, cols=2 * CW):
                for k in range(k0, k0 + n):
                    u = 4 * q + k
                    act.wait_ge(w_landed[k % RING], 16 * (q + k // RING) + 16)
                    if not (isinstance(u, int) and u < RING):
                        act.wait_ge(unit_used, u - RING + 1)
                    src = w_raw[:, k % RING, :, :].rearrange("p a n -> p (a n)")[:, 0:cols]
                    dst = w_hi[:, k % RING, :, :].rearrange("p a n -> p (a n)")[:, 0:cols]
                    f(dst, src).then_inc(w_hi_done, 1)
                    if after:
                        after(k - k0)

            def hi_part(name, n, o, i):
                act.wait_ge(fam[name][0], n)
                f(o, i).then_inc(fam[name][1], 1)

            def summed(q, k_end):
                act.wait_ge(unit_used, 4 * q + k_end)

            def root(stage, o, mean, eps):
                act.wait_ge(sq_used, SQ_DONE[stage])
                f(o, mean, ACT.Sqrt, bias=eps).then_inc(std_ready, 1)

            for j in range(NQ):
                act.wait_ge(xt_done, j + 1)
                f(xT0[:, 4 * j:4 * j + 4, :], acc[j % 2][:, :, :])
                if j == NQ - 1:
                    act.wait_ge(sq_added, 1)
                f(sq0[:, j % 2] if j else sqs0, acc[j % 2][:, :, :], ACT.Square).then_inc(sq_ready, 1)
                if j == 2:
                    act.wait_ge(vecs_t, 1)
                    f(vecs[:, 0:V_SSM], bank5[:, 0:V_SSM])
                    f(vecs[:, V_SSM:N_VECS], bank5[:, V_SSM:N_VECS], scale=0.5)
                    f(cwb[:, :], bank5[:, N_VECS:N_VECS + (TAPS + 1) * NCB], scale=0.5).then_inc(vecs_ready, 1)
            act.wait_ge(sq_ready, NQ)
            act.dma_start(xT_dram, xT0[:, :, :]).then_inc(xT_stored, 16)
            hi_units(Q_B0, 0, 3)
            root(RMS_X, rstd0[:, :], bank4[:, 0:T], EPS)
            for k in range(PIECES):
                hi_part("op_h", k + 1, h_hi[:, 2 * k:2 * k + 2, :], hf0[:, k % 4])
                if 1 <= k < PIECES - 2:
                    hi_units(Q_B0, k + 2, 1)
            hi_units(Q_DT, 0, 4, cols=CW)
            f(head_col[0:NH, 2:3], head_col[0:NH, 1:2], ACT.Exp).then_inc(dt_exp, 1)

            def conv_take(n, q, k_end, accum):
                summed(q, k_end)
                if not (isinstance(n, int) and n == 0):
                    act.wait_ge(conv_out, n)
                f(xraw[:, :, :], accum[:, :, :]).then_inc(acc_taken, 1)

            def conv_tanhs(n):
                act.wait_ge(conv_acc, CONV_STEPS * (n + 1))
                f(xraw[:, :, :], xs[:, :, :], ACT.Tanh).then_inc(conv_tanh, 1)

            def softplus(c, k):
                if c == 1 and k == 4:
                    act.wait_ge(dt_steps, 2)
                    f(dt_e[0:NH, :], dt_r[0:NH, :], ACT.Exp, scale=-1.0).then_inc(dt_exp, 1)
                if c == 1 and k == 5:
                    act.wait_ge(dt_steps, 3)
                    f(dt_ln[0:NH, :], dt_u[0:NH, :], ACT.Ln).then_inc(dt_log, 1)
                if c == 2 and k == 1:
                    act.wait_ge(dt_steps, DT_STEPS)
                    act.dma_start(cum_dram, cum_T[0:NH, :]).then_inc(cum_stored, 16)

            for c in range(1, 4):
                def conv_before(k):
                    softplus(c, k)
                    if k == 3:
                        conv_take(c - 1, Q_BC + 2 * c, 0, acc[(c - 1) % 2])
                    if k == 7:
                        conv_tanhs(c - 1)
                hi_units(Q_BC + 2 * c, 0, 8, after=conv_before)

            def falls(p_, i):
                for r in range(HEADS):
                    o = decay[:, r, CH * i:CH * i + CH]
                    last = f(o, o, ACT.Relu, scale=-1.0, bias=tok_cum[:, i, ds(HEADS * p_ + r, 1)])
                return last

            def scan_part(k, p_, q):
                if k == 0:
                    act.wait_ge(cb_done, p_ + 1)
                    f(bn[:, :], bank5[:, 0:CH]).then_inc(bn_taken, 1)
                    act.wait_ge(cum_landed, 48 * (p_ + 1))
                    falls(p_, 1)
                if k == 1:
                    act.wait_ge(end_ready, p_ + 1)
                    falls(p_, 0).then_inc(fall_ready, 1)
                if k == 2:
                    f(to_end[:, :], to_end[:, :], ACT.Exp)
                    f(ecum[:, :, :], ecum[:, :, :], ACT.Exp)
                    act.wait_ge(fall_ready, p_ + 1)
                    f(decay[:, :, :], decay[:, :, :], ACT.Exp, scale=-1.0).then_inc(decay_ready, 1)
                if k == 3:
                    summed(q, 0)
                    f(zraw[:, :, :], acc[1][:, :, :])
                    f(ztanh[:, :, :], acc[1][:, :, :], ACT.Tanh, scale=0.5).then_inc(acc_taken, 1)
                if k == 6:
                    act.wait_ge(state_done, p_ + 1)
                    f(state[:, :], bank4[:, :]).then_inc(state_ready, 1)
                if k == 10:
                    act.wait_ge(y_gated, p_ + 1)
                    f(ztanh[:, :, :], yg[:, :, :], ACT.Square).then_inc(ysq_ready, 1)
                if k == 13:
                    act.wait_ge(yss_done, p_ + 1)
                    f(yrstd[:, :], pair[:, 0, :], ACT.Sqrt, bias=EPS).then_inc(ystd_ready, 1)
                if k == 14:
                    hi_part("op_y", p_ + 1, y_hi[:, ds(4 * p_, 4), :], yg[:, :, :])

            def group(g, lag):
                q = Q_SSD + 4 * g

                def at(k):
                    if lag:
                        scan_part(k, g - 1, q)
                    elif k == 3:
                        conv_take(3, q, 0, acc[1])
                    elif k == 7:
                        conv_tanhs(3)
                    if k == 8:
                        act.wait_ge(conv_out, 4)
                        if lag:
                            act.wait_ge(cb_done, g)
                        f(b_own[:, :], bc[:, ds(g, 1), :].rearrange("p a t -> p (a t)")).then_inc(b_ready, 1)
                    if k == 11:
                        conv_take(4 + g, q, 8, acc[0])
                    if k == 13:
                        conv_tanhs(4 + g)
                hi_units(q, 0, 16, after=at)

            act.wait_ge(tok_ready, 1)
            act.wait_ge(xT_stored, 16)
            group(0, False)
            with act.Fori(1, GROUPS) as g:
                group(g, True)

            def pooling(k):
                if k < 16:
                    scan_part(k, GROUPS - 1, Q_POOL)
                for m in range(4):
                    if k == 8 * m + 11:
                        summed(Q_POOL, 8 * m + 8)
                        if m:
                            act.wait_ge(fam["op_pool"][0], m)
                        else:
                            act.wait_ge(y_gated, GROUPS)
                        f(uraw[:, :, :], acc[m % 2][:, :, :]).then_inc(acc_taken, 1)
                    if k == (16, 23, 31, 38)[m]:
                        if m == 2:
                            act.wait_ge(fam["op_y"][2], GROUPS)
                        hi_part("op_pool", m + 1, pool_hi[m], windows_of(csum, m))
                    if k == (37, 38, 40, 42)[m]:
                        summed(Q_POOL, 34 + 2 * m)
                        if m:
                            act.wait_ge(fam["op_yp"][2], m)
                        for n in range(NB):
                            col = V_POOL + NB * m + n
                            last = f(ypf[:, n, :], acc[m % 2][:, n, :], scale=vecs[:, col:col + 1])
                        last.then_inc(acc_taken, 1)
                        act.wait_ge(acc_taken, C_POOL + 4 + m + 1)
                        f(yp_hi[:, NB * m:NB * m + NB, :], ypf[:, :, :]).then_inc(fam["op_yp"][1], 1)
            hi_units(Q_POOL, 0, 40, after=pooling)

            def gate_take(m, q):
                summed(q, 8)
                if not (isinstance(m, int) and m == 0):
                    act.wait_ge(merged, m)
                f(gate[:, :, :], acc[0][:, :, :], ACT.Tanh, scale=0.5).then_inc(acc_taken, 1)

            def prod_take(m, q):
                summed(q, 0)
                f(prod[:, :, :], acc[1][:, :, :]).then_inc(acc_taken, 1)

            def po(j, q, first):
                def at(k):
                    if first:
                        pooling(40 + k)
                    if not first and k == 3:
                        prod_take(j - 1, q)
                    if k == 11:
                        gate_take(j, q)
                hi_units(q, 0, 16, after=at)

            po(0, Q_PO, True)
            with act.Fori(1, NQ) as j:
                po(j, Q_PO + 4 * j, False)

            def so(j, q, first):
                def at(k):
                    if k == 3:
                        prod_take(NQ + j - 1, q)
                    if k == 6 and not first:
                        hi_part("op_m", j, m_hi[:, ds(4 * (j - 1), 4), :], prod[:, :, :])
                    if k == 11:
                        gate_take(NQ + j, q)
                hi_units(q, 0, 24, after=at)

            so(0, Q_SO, True)
            with act.Fori(1, NQ) as j:
                so(j, Q_SO + 6 * j, False)

            def post_take(stage, j, q, k_end, accum, first, squares, gain, between=None):
                summed(q, k_end)
                if j == NQ - 1:
                    act.wait_ge(sq_added, SQ_ADDED[stage] + 1)
                f(squares[:, j % 2] if j else first, accum[:, :, :], ACT.Square).then_inc(sq_ready, 1)
                if between:
                    between()
                for n in range(NB):
                    col = gain + NB * j + n
                    last = f(fg[:, NB * j + n, :], accum[:, n, :], scale=vecs[:, col:col + 1])
                last.then_inc(acc_taken, 1)

            for j in range(NQ):
                q = Q_MIX + 2 * j

                def at(k):
                    if j == 0 and k == 3:
                        prod_take(2 * NQ - 1, q)
                    if j == 0 and k == 6:
                        hi_part("op_m", NQ, m_hi[:, KB - NB:KB, :], prod[:, :, :])
                    if j > 0 and k == 3:
                        if j == 1:
                            act.wait_ge(fam["op_m"][2], NQ)
                        post_take(RMS_MIX, j - 1, q, 0, acc[(j - 1) % 2], sqs1, sq1, V_POST_MIX)
                hi_units(q, 0, 8, after=at)

            def last_quarter(half, ready, count):
                act.wait_ge(ready, count)
                act.wait_ge(sq_added, SQ_ADDED[RMS_MIX] + 1)
                blocks = slice(2 * half, 2 * half + 2)
                f(sq1[:, (NQ - 1) % 2, blocks], acc[1][:, blocks, :],
                  ACT.Square).then_inc((sq_half, sq_ready)[half], 1)
                if half:
                    root(RMS_MIX, rstd1[:, :], bank4[:, 0:T], 4 * EPS)
                for n in (2 * half, 2 * half + 1):
                    b = NB * (NQ - 1) + n
                    last = f(fg[:, b, :], acc[1][:, n, :], scale=vecs[:, V_POST_MIX + b:V_POST_MIX + b + 1])
                return last

            last_quarter(0, half_done, 1)
            hi_units(Q_FF, 0, 3)
            last_quarter(1, unit_used, 4 * Q_FF).then_inc(acc_taken, 1)
            hi_units(Q_FF, 3, 1)

            def x1_operand(k):
                act.wait_ge(x1_ready, k + 1)
                if k >= 4:
                    act.wait_ge(fam["op_h"][2], PIECES + k - 3)
                for n in range(2):
                    b = 2 * k + n
                    last = f(hf1[:, k % 4, n, :], xT[:, b, :], scale=vecs[:, V_PRE_FFN + b:V_PRE_FFN + b + 1])
                last.then_inc(fam["op_h"][0], 1)
                hi_part("op_h", PIECES + k + 1, h_hi[:, 2 * k:2 * k + 2, :], hf1[:, k % 4])

            def x1_square(j):
                act.wait_ge(sq_used, SQ_DONE[RMS_MIX] + max(0, j - 1))
                f(sq1[:, j % 2], xT[:, NB * j:NB * j + NB, :], ACT.Square).then_inc(sq_ready, 1)

            for k in range(PIECES):
                x1_operand(k)
                if k % 2:
                    x1_square(k // 2)
                if k >= 2:
                    hi_units(Q_FF, k + 2, 1)
            hi_units(Q_FF, 10, 1)
            root(RMS_X1, rstd2[:, :], bank5[:, 0:T], EPS)

            def ff(j, k, q, lag):
                if lag and k == 6:
                    hi_part("op_ff", j, act_hi[:, ds(4 * (j - 1), 4), :], uff[:, :, :])
                if k == 12:
                    act.wait_ge(acc_taken, C_FF + 2 * j + 1)
                    f(tg[:, :, :], graw[:, :, :], ACT.Tanh, scale=0.5).then_inc(gtanh_ready, 1)

            def first_ff(k):
                k += 11
                ff(0, k, Q_FF, False)
                if k == 14:
                    act.wait_ge(pt_done, 1)
                    f(pf[:, :, :], pair[:, 0:2, :]).then_inc(fam["op_p"][0], 1)
                    hi_part("op_p", 1, p_hi[:, :, :], pf[:, :, :])
            hi_units(Q_FF, 11, 5, after=first_ff)
            with act.Fori(1, NFF) as j:
                hi_units(Q_FF + 4 * j, 0, 16, after=lambda k: ff(j, k, Q_FF + 4 * j, True))

            for t in range(2):
                for i in range(2):
                    j, q = 2 * t + i, Q_FO + t * (FO_UNITS // 2)

                    def at(k):
                        if j == 0 and k < 8:
                            ff(NFF, k, q, True)
                        if j > 0 and k == 3:
                            if j == 1:
                                act.wait_ge(fam["op_ff"][2], NFF)
                            post_take(RMS_F, j - 1, q, FO_UNITS * i, acc[1 - i], sqs_f, sq_f, V_POST_FFN)
                    hi_units(q, FO_UNITS * i, FO_UNITS, after=at)

            def ple_take(c):
                summed(Q_PP, c + 1)
                f(ple[:, NB * c:NB * c + NB, :], acc[c % 2][:, :, :], scale=0.5).then_inc(acc_taken, 1)

            hi_units(Q_PP, 0, 3)
            post_take(RMS_F, NQ - 1, Q_PP, 0, acc[1], sqs_f, sq_f, V_POST_FFN,
                      between=lambda: root(RMS_F, rstd_f[:, :], bank4[:, 0:T], 4 * EPS))
            hi_units(Q_PP, 3, 1)
            for k in range(PIECES):
                if k < NQ:
                    ple_take(k)
                hi_part("op_x2", k + 1, h_hi[:, 2 * k:2 * k + 2, :], xT[:, 2 * k:2 * k + 2, :])
                hi_units(Q_PG, k, 1)

            def tgate_take(j, q):
                summed(q, 0)
                if j:
                    act.wait_ge(o_ready, j)
                f(tgate[:, :, :], acc[j % 2][:, :, :], ACT.Tanh, scale=0.5).then_inc(acc_taken, 1)

            def rows_take(j):
                act.wait_ge(ot_done, j + 1)
                f(o_rows[:, :, CW * j:CW * j + CW],
                  pair[:, :, :].rearrange("p (a b) t -> p a (b t)", a=2)).then_inc(rows_ready, 1)

            for j in range(1, NQ):
                def at(k):
                    if k == 3:
                        tgate_take(j - 1, Q_PG + 2 * j)
                    if k == 7:
                        rows_take(j - 1)
                hi_units(Q_PG + 2 * j, 0, 8, after=at)
            act.wait_ge(o_ready, NQ - 1)
            for half, ready, count in ((0, half_done, 2), (1, unit_used, 4 * (Q_PG + 2 * NQ))):
                act.wait_ge(ready, count)
                blocks = slice(2 * half, 2 * half + 2)
                f(tgate[:, blocks, :], acc[1][:, blocks, :], ACT.Tanh, scale=0.5).then_inc(last_gate, 1)
            act.wait_ge(ot_done, NQ)
            f(o_rows[:, :, CW * (NQ - 1):D - CW // 2], pair[:, 0:2, :]).then_inc(rows_ready, 1)

        @block.vector
        def _(dve):
            v = nc.vector

            def lo_units(q, k0, n, after=None, cols=2 * CW):
                for k in range(k0, k0 + n):
                    dve.wait_ge(w_hi_done, 4 * q + k + 1)
                    raw, high, low = (t[:, k % RING, :, :].rearrange("p a n -> p (a n)")[:, 0:cols]
                                      for t in (w_raw, w_hi, w_lo))
                    v.tensor_tensor(low, raw, high.bitcast(F32), ALU.subtract).then_inc(w_lo_done, 1)
                    if after:
                        after(k - k0)

            def lo_part(name, n, o, i, high):
                dve.wait_ge(fam[name][1], n)
                v.tensor_tensor(o, i, high.bitcast(F32), ALU.subtract).then_inc(fam[name][2], 1)

            def inverse(stage, o):
                dve.wait_ge(std_ready, stage + 1)
                v.reciprocal(o, o).then_inc(rstd_ready, 1)
                dve.wait_ge(rstd_ready, stage + 1)

            def h_low(n0, k, hf):
                two = slice(2 * k, 2 * k + 2)
                lo_part("op_h", n0 + k + 1, h_lo[:, two, :], hf[:, k % 4], h_hi[:, two, :])

            def add_squares(stage, j, total, squares):
                dve.wait_ge(sq_ready, NQ * stage + j + 1)
                if j == 2:
                    dve.wait_ge(sq_added, SQ_ADDED[stage] + 1)
                v.tensor_tensor(total[:, :, :], total[:, :, :], squares[:, j % 2], ALU.add).then_inc(sq_added, 1)

            dve.wait_ge(consts, N_CONSTS)
            for j in (1, 2):
                add_squares(RMS_X, j, sqs0, sq0)
            dve.wait_ge(vec_landed, 16 * 12)
            by_half = dsk_row[:, :].rearrange("p (b h) -> p b h", h=2)
            for half in range(2):
                rows = slice(HD * half, HD * half + HD)
                v.tensor_copy(skip[rows, :], by_half[rows, :, half])
            lo_units(Q_B0, 0, 3)
            inverse(RMS_X, rstd0[:, :])
            dve.wait_ge(vecs_ready, 1)

            def x0_piece(k):
                if k >= 4:
                    dve.wait_ge(fam["op_h"][2], k - 3)
                for n in range(2):
                    b = 2 * k + n
                    last = v.scalar_tensor_tensor(hf0[:, k % 4, n, :], xT0[:, b, :],
                                                  vecs[:, V_PRE_MIX + b:V_PRE_MIX + b + 1],
                                                  rstd0[:, :], ALU.mult, ALU.mult)
                last.then_inc(fam["op_h"][0], 1)

            x0_piece(0)
            for k in range(PIECES):
                if k + 1 < PIECES:
                    x0_piece(k + 1)
                h_low(0, k, hf0)
                if 1 <= k < PIECES - 2:
                    lo_units(Q_B0, k + 2, 1)
            lo_units(Q_DT, 0, 4, cols=CW)

            steps = Chain(dve, dt_steps)
            H = slice(0, NH)

            def softplus(k):
                if k == 3:
                    dve.wait_ge(unit_used, 4 * Q_DT + 4)
                    steps.step(v.tensor_scalar(dt_v[H, :], bank4[H, T:2 * T], head_col[H, 0:1], None, ALU.add))
                    steps.wait()
                    steps.step(v.scalar_tensor_tensor(dt_r[H, :], dt_v[H, :], -1.0, dt_v[H, :], ALU.mult, ALU.max))
                if k == 4:
                    dve.wait_ge(dt_exp, 2)
                    steps.step(v.tensor_scalar(dt_u[H, :], dt_e[H, :], 1.0, None, ALU.add))
                if k == 5:
                    dve.wait_ge(dt_log, 1)
                    steps.step(v.tensor_scalar(dt_r[H, :], dt_u[H, :], -1.0, None, ALU.add))
                    steps.wait()
                    steps.step(v.tensor_tensor(dt_e[H, :], dt_e[H, :], dt_r[H, :], ALU.subtract))
                    steps.wait()
                    steps.step(v.reciprocal(dt_r[H, :], dt_u[H, :]))
                if k == 6:
                    steps.wait()
                    steps.step(v.tensor_tensor(dt_e[H, :], dt_e[H, :], dt_r[H, :], ALU.mult))
                    steps.wait()
                    steps.step(v.tensor_tensor(dt_ln[H, :], dt_ln[H, :], dt_e[H, :], ALU.add))
                    steps.wait()
                    steps.step(v.scalar_tensor_tensor(dt_T[H, :], dt_v[H, :], 0.0, dt_ln[H, :], ALU.max, ALU.add))
                    steps.wait()
                    steps.step(v.tensor_scalar(dt_a[H, :], dt_T[H, :], head_col[H, 2:3], -1.0, ALU.mult, ALU.mult))
                    steps.wait()
                    for i in range(2):
                        c = slice(CH * i, CH * i + CH)
                        steps.step(v.tensor_tensor_scan(cum_T[H, c], ones[H, 0:CH], dt_a[H, c], 0.0, ALU.mult, ALU.add))
                    assert steps.n == DT_STEPS

            def by_token(c, k):
                if c == 2 and k == 6:
                    dve.wait_ge(tok_done, 1)
                    v.tensor_copy(tok_dt[:, :, :], bank5[:, 0:2 * NH].rearrange("p (c h) -> p c h", h=NH))
                    v.tensor_copy(tok_cum[:, :, :],
                                  bank5[:, 2 * NH:4 * NH].rearrange("p (c h) -> p c h", h=NH)).then_inc(tok_ready, 1)

            def conv_blocks(n, c, block0, pair_):
                if pair_ == 0:
                    dve.wait_ge(acc_taken, c + 1)
                chain = Chain(dve, conv_acc, CONV_STEPS * n + 8 * pair_)
                col = lambda tap, b: cwb[:, ds(NCB * tap + block0 + b, 1)]
                for t in range(TAPS):
                    for b in (2 * pair_, 2 * pair_ + 1):
                        if t == 0:
                            chain.step(v.tensor_scalar(xs[:, b, :], xraw[:, b, :], col(TAPS - 1, b), col(TAPS, b),
                                                       ALU.mult, ALU.add))
                        else:
                            chain.wait(chain.n - 1)
                            chain.step(v.scalar_tensor_tensor(xs[:, b, t:T], xraw[:, b, 0:T - t], col(TAPS - 1 - t, b),
                                                              xs[:, b, t:T], ALU.mult, ALU.add))
                assert chain.n == CONV_STEPS // 2

            def conv_end(n, o):
                dve.wait_ge(conv_tanh, n + 1)
                v.scalar_tensor_tensor(o, xraw[:, :, :], 1.0, xs[:, :, :], ALU.add, ALU.mult).then_inc(conv_out, 1)

            def conv_bc(n, k):
                if k == 3 or k == 4:
                    conv_blocks(n, C_BC + n, DI // P + NB * n, k - 3)
                if k == 7:
                    conv_end(n, bc[:, ds(NB * n, NB), :])

            for c in range(1, 4):
                def at(k):
                    if c == 1:
                        softplus(k)
                    by_token(c, k)
                    conv_bc(c - 1, k)
                lo_units(Q_BC + 2 * c, 0, 8, after=at)

            def scan_part(k, p_, z_chunk):
                heads = ds(HEADS * p_, HEADS)
                if k == 0:
                    dve.wait_ge(cb_done, p_ + 1)
                    v.tensor_tensor(cbm[:, :, :], bank4[:, 0:2 * CH].rearrange("p (c t) -> p c t", t=CH),
                                    mask[:, :].unsqueeze(1).to_broadcast([P, 2, CH]), ALU.mult).then_inc(cb_taken, 1)
                    dve.wait_ge(cum_landed, 48 * (p_ + 1))
                    v.tensor_tensor(to_end[:, :], decay[:, :, CH - 1], tok_cum[:, 0, heads],
                                    ALU.subtract).then_inc(end_ready, 1)
                if k == 3:
                    dve.wait_ge(decay_ready, p_ + 1)
                    dve.wait_ge(cb_taken, p_ + 1)
                    both = cbm[:, :, :].rearrange("p c t -> p (c t)").unsqueeze(1).to_broadcast([P, HEADS, T])
                    v.tensor_tensor(decay[:, :, :], decay[:, :, :], both, ALU.mult).then_inc(w_ready, 1)
                if k == 2:
                    dve.wait_ge(xtr_done, p_ + 1)
                    for i, bank in enumerate((bank4, bank5)):
                        v.tensor_tensor(xdt[:, i, :, :], bank[:, :].rearrange("p (h d) -> p h d", d=HD),
                                        tok_dt[:, i, heads].unsqueeze(2).to_broadcast([P, HEADS, HD]),
                                        ALU.mult).then_inc(xdt_ready, 1)
                if k == 3:
                    dve.wait_ge(xdt_ready, 2 * p_ + 1)
                    v.tensor_tensor(xend[:, :, :], xdt[:, 0, :, :], to_end[:, :].unsqueeze(2).to_broadcast([P, HEADS, HD]),
                                    ALU.mult).then_inc(xend_ready, 1)
                chain = Chain(dve, y_steps, Y_STEPS * p_)
                if k == 5:
                    dve.wait_ge(acc_taken, z_chunk + 1)
                    chain.step(v.scalar_tensor_tensor(zraw[:, :, :], ztanh[:, :, :], 1.0, zraw[:, :, :], ALU.add, ALU.mult))
                if k == 8:
                    chain.n = 1
                    chain.wait()
                    dve.wait_ge(y_done, p_ + 1)
                    for n in range(NB):
                        chain.step(v.scalar_tensor_tensor(yg[:, n, :], xs[:, n, :], skip[:, ds(NB * p_ + n, 1)],
                                                          pair[:, n, :], ALU.mult, ALU.add))
                    chain.step(v.tensor_tensor(ztanh[:, :, 0:CH], bank5[:, :].rearrange("p (b t) -> p b t", t=CH),
                                               ecum[:, :, :], ALU.mult))
                    chain.wait()
                    chain.step(v.tensor_tensor(yg[:, :, CH:T], yg[:, :, CH:T], ztanh[:, :, 0:CH], ALU.add))
                    assert chain.n == Y_STEPS
                if k == 9:
                    dve.wait_ge(y_steps, Y_STEPS * (p_ + 1))
                    v.tensor_tensor(yg[:, :, :], yg[:, :, :], zraw[:, :, :], ALU.mult).then_inc(y_gated, 1)
                if k == 11:
                    dve.wait_ge(ysq_ready, p_ + 1)
                    v.tensor_reduce(ysum[:, :], ztanh[:, :, :].rearrange("p b t -> p t b"), axis=AX.X,
                                    op=ALU.add).then_inc(ysum_ready, 1)
                if k == 13:
                    dve.wait_ge(ystd_ready, p_ + 1)
                    v.reciprocal(yrstd[:, :], yrstd[:, :]).then_inc(yrstd_ready, 1)
                    dve.wait_ge(yrstd_ready, p_ + 1)
                    for n in range(NB):
                        last = v.scalar_tensor_tensor(yg[:, n, :], yg[:, n, :], vecs[:, ds(V_SSM + NB * p_ + n, 1)],
                                                      yrstd[:, :], ALU.mult, ALU.mult)
                    last.then_inc(fam["op_y"][0], 1)
                if k == 15:
                    four = ds(NB * p_, NB)
                    lo_part("op_y", p_ + 1, y_lo[:, four, :], yg[:, :, :], y_hi[:, four, :])

            def group(g, lag):
                def at(k):
                    if lag:
                        scan_part(k, g - 1, C_SSD + 2 * g - 1)
                    else:
                        conv_bc(3, k)
                    if k == 11 or k == 12:
                        conv_blocks(4 + g, C_SSD + 2 * g, NB * g, k - 11)
                    if k == 14:
                        conv_end(4 + g, xs[:, :, :])
                lo_units(Q_SSD + 4 * g, 0, 16, after=at)

            dve.wait_ge(tok_ready, 1)
            group(0, False)
            with dve.Fori(1, GROUPS) as g:
                group(g, True)

            def windows(m):
                w, means = WINDOWS[m], windows_of(csum, m)
                chain = Chain(dve, pool_steps, POOL_STEPS * m)
                if m:
                    dve.wait_ge(fam["op_pool"][2], m)
                chain.step(v.memset(csum[:, :, 0:16], 0.0))
                dve.wait_ge(acc_taken, C_POOL + m + 1)
                for n in range(NB):
                    chain.step(v.tensor_tensor_scan(csum[:, n, 16:16 + T], ones[:, 0:1].to_broadcast([P, T]),
                                                    uraw[:, n, :], 0.0, ALU.mult, ALU.add))
                chain.wait()
                chain.step(v.tensor_tensor(means, csum[:, :, 16:16 + T], means, ALU.subtract))
                chain.wait()
                chain.step(v.scalar_tensor_tensor(means[:, :, 16:T], means[:, :, 16:T], 1.0 / w, uraw[:, :, 16:T],
                                                  ALU.mult, ALU.subtract))
                chain.step(v.tensor_tensor(means[:, :, 0:16], means[:, :, 0:16],
                                           inv_n[:, m, :].unsqueeze(1).to_broadcast([P, NB, 16]), ALU.mult))
                chain.wait()
                v.tensor_tensor(means[:, :, 0:16], means[:, :, 0:16], uraw[:, :, 0:16],
                                ALU.subtract).then_inc(fam["op_pool"][0], 1)
                assert chain.n == POOL_STEPS

            def pooling(k):
                if k < 16:
                    scan_part(k, GROUPS - 1, C_POOL - 1)
                for m in range(4):
                    if k == (14, 21, 29, 35)[m]:
                        if m == 0:
                            dve.wait_ge(ysum_ready, GROUPS)
                        windows(m)
                    if k == (16, 23, 31, 38)[m]:
                        lo_part("op_pool", m + 1, pool_lo[m], windows_of(csum, m), pool_hi[m])
                    if k == (37, 39, 41, 43)[m]:
                        four = slice(NB * m, NB * m + NB)
                        lo_part("op_yp", m + 1, yp_lo[:, four, :], ypf[:, :, :], yp_hi[:, four, :])
            lo_units(Q_POOL, 0, 40, after=pooling)

            def merge(m, j, own):
                dve.wait_ge(acc_taken, C_PO + 2 * m + 2)
                dst = prod[:, :, :] if own else mpool[:, ds(NB * j, NB), :]
                v.scalar_tensor_tensor(dst, gate[:, :, :], 1.0, prod[:, :, :], ALU.add, ALU.mult).then_inc(merged, 1)
                if own:
                    dve.wait_ge(merged, m + 1)
                    v.tensor_tensor(dst, dst, mpool[:, ds(NB * j, NB), :], ALU.add).then_inc(fam["op_m"][0], 1)

            def m_low(j):
                four = ds(NB * j, NB)
                lo_part("op_m", j + 1, m_lo[:, four, :], prod[:, :, :], m_hi[:, four, :])

            def po(j, q, first):
                def at(k):
                    if first:
                        pooling(40 + k)
                    if not first and k == 4:
                        merge(j - 1, j - 1, False)
                lo_units(q, 0, 16, after=at)

            po(0, Q_PO, True)
            with dve.Fori(1, NQ) as j:
                po(j, Q_PO + 4 * j, False)

            def so(j, q, first):
                def at(k):
                    if k == 4:
                        if first:
                            merge(NQ - 1, NQ - 1, False)
                        else:
                            merge(NQ + j - 1, j - 1, True)
                    if k == 6 and not first:
                        m_low(j - 1)
                lo_units(q, 0, 24, after=at)

            so(0, Q_SO, True)
            with dve.Fori(1, NQ) as j:
                so(j, Q_SO + 6 * j, False)

            def last_merge(k):
                if k == 4:
                    merge(2 * NQ - 1, NQ - 1, True)
                if k == 6:
                    m_low(NQ - 1)
            lo_units(Q_MIX, 0, 8, after=last_merge)
            for j in range(1, NQ):
                lo_units(Q_MIX + 2 * j, 0, 8,
                         after=lambda k: j > 1 and k == 5 and add_squares(RMS_MIX, j - 1, sqs1, sq1))

            def residual(n, k, x_, rstd, ready):
                two = slice(2 * k, 2 * k + 2)
                v.tensor_tensor(fg[:, two, :], fg[:, two, :], rstd.unsqueeze(1).to_broadcast([P, 2, T]),
                                ALU.mult).then_inc(res_steps, 1)
                dve.wait_ge(res_steps, PIECES * n + k + 1)
                v.tensor_tensor(xT[:, two, :], x_[:, two, :], fg[:, two, :], ALU.add).then_inc(ready, 1)

            lo_units(Q_FF, 0, 3)
            inverse(RMS_MIX, rstd1[:, :])
            dve.wait_ge(xT_landed, 16)
            residual(0, 0, x_back, rstd1[:, :], x1_ready)
            for k in range(PIECES):
                if k + 1 == PIECES - 2:
                    dve.wait_ge(acc_taken, C_FF)
                if k + 1 < PIECES:
                    residual(0, k + 1, x_back, rstd1[:, :], x1_ready)
                h_low(PIECES, k, hf1)
                if k:
                    lo_units(Q_FF, k + 2, 1)

            def ff(j, k, lag):
                by_token = rstd2[:, :].unsqueeze(1).to_broadcast([P, NB, T])
                if lag and k == 3:
                    dve.wait_ge(unit_used, 4 * (Q_FF + 4 * j))
                    v.tensor_tensor(uff[:, :, :], acc[1][:, :, :], by_token, ALU.mult).then_inc(acc_taken, 1)
                if lag and k == 4:
                    dve.wait_ge(acc_taken, C_FF + 2 * j)
                    dve.wait_ge(gg_ready, j)
                    v.tensor_tensor(uff[:, :, :], uff[:, :, :], graw[:, :, :], ALU.mult).then_inc(fam["op_ff"][0], 1)
                if lag and k == 6:
                    four = ds(NB * (j - 1), NB)
                    lo_part("op_ff", j, act_lo[:, four, :], uff[:, :, :], act_hi[:, four, :])
                if k == 11:
                    dve.wait_ge(unit_used, 4 * (Q_FF + 4 * j) + 8)
                    if lag:
                        dve.wait_ge(fam["op_ff"][0], j)
                    v.tensor_tensor(graw[:, :, :], acc[0][:, :, :], by_token, ALU.mult).then_inc(acc_taken, 1)
                if k == 13:
                    dve.wait_ge(gtanh_ready, j + 1)
                    v.scalar_tensor_tensor(graw[:, :, :], tg[:, :, :], 1.0, graw[:, :, :],
                                           ALU.add, ALU.mult).then_inc(gg_ready, 1)

            def first_ff(k):
                if k + 10 == 11:
                    inverse(RMS_X1, rstd2[:, :])
                ff(0, k + 10, False)
                if k + 10 == 15:
                    lo_part("op_p", 1, p_lo[:, :, :], pf[:, :, :], p_hi[:, :, :])
            lo_units(Q_FF, 10, 6, after=first_ff)
            with dve.Fori(1, NFF) as j:
                lo_units(Q_FF + 4 * j, 0, 16, after=lambda k: ff(j, k, True))

            lo_units(Q_FO, 0, FO_UNITS, after=lambda k: k < 8 and ff(NFF, k, True))
            lo_units(Q_FO, FO_UNITS, FO_UNITS)
            for j in (2, 3):
                lo_units(Q_FO + FO_UNITS // 2, (j - 2) * FO_UNITS, FO_UNITS,
                         after=lambda k: k == 5 and add_squares(RMS_F, j - 1, sqs_f, sq_f))

            def x2_lo(k):
                two = slice(2 * k, 2 * k + 2)
                lo_part("op_x2", k + 1, h_lo[:, two, :], xT[:, two, :], h_hi[:, two, :])

            lo_units(Q_PP, 0, 3)
            inverse(RMS_F, rstd_f[:, :])
            for k in range(PIECES):
                if k == PIECES - 2:
                    dve.wait_ge(acc_taken, C_PP)
                residual(1, k, xT, rstd_f[:, :], fam["op_x2"][0])
                if k == 0:
                    lo_units(Q_PP, 3, 1)
                else:
                    x2_lo(k - 1)
                    lo_units(Q_PG, k - 1, 1)
            x2_lo(PIECES - 1)
            lo_units(Q_PG, PIECES - 1, 1)

            def output(j):
                four = slice(NB * j, NB * j + NB)
                dve.wait_ge(acc_taken, C_PG + j + 1)
                if j:
                    dve.wait_ge(ot_done, j)
                v.scalar_tensor_tensor(o_T[:, :, :], tgate[:, :, :], 1.0, ple[:, four, :],
                                       ALU.add, ALU.mult).then_inc(o_steps, 1)
                dve.wait_ge(o_steps, j + 1)
                v.tensor_tensor(o_T[:, :, :], o_T[:, :, :], xT[:, four, :], ALU.add).then_inc(o_ready, 1)

            for j in range(1, NQ):
                lo_units(Q_PG + 2 * j, 0, 8, after=lambda k: k == 3 and output(j - 1))
            for half in range(2):
                dve.wait_ge(last_gate, half + 1)
                if half == 0:
                    dve.wait_ge(ot_done, NQ - 1)
                b = slice(2 * half, 2 * half + 2)
                four = slice(NB * (NQ - 1) + 2 * half, NB * (NQ - 1) + 2 * half + 2)
                v.scalar_tensor_tensor(o_T[:, b, :], tgate[:, b, :], 1.0, ple[:, four, :],
                                       ALU.add, ALU.mult).then_inc(o_steps, 1)
                dve.wait_ge(o_steps, NQ + half)
                v.tensor_tensor(o_T[:, b, :], o_T[:, b, :], xT[:, four, :], ALU.add).then_inc(o_ready, 1)
            dve.wait_ge(ot_done, NQ + 1)
            v.tensor_copy(o_rows[:, :, D - CW // 2:D], pair[:, 2:4, :]).then_inc(rows_late, 1)


_INS = ["x", "p", "w_in", "conv_w", "conv_b", "dt_bias", "a_log", "d_skip", "ssm_norm_g", "w_ssm_out",
        "w_pool_grp", "pool_scale", "w_pool_out", "w_mix_out", "g_pre_mix", "g_post_mix",
        "g_pre_ffn", "g_post_ffn", "w_ffn_in", "w_ffn_out", "w_ple_proj", "w_ple_gate"]


def kernel(**inputs):
    import numpy as _np
    import concourse.bacc as _bacc
    from concourse import mybir as _mybir
    from concourse.bass_utils import run_bass_kernel_spmd as _run

    nc = _bacc.Bacc("TRN2", target_bir_lowering=False, num_devices=1)
    arrays, args = {}, []
    for name in _INS:
        a = _np.ascontiguousarray(inputs[name])
        arrays[f"in_{name}_dram"] = a
        args.append(nc.dram_tensor(f"in_{name}_dram", a.shape, _mybir.dt.from_np(a.dtype), kind="ExternalInput").ap())
    args.append(nc.dram_tensor("out_dram", (1, T, D), F32, kind="ExternalOutput").ap())
    build(nc, *args)
    r = _run(nc, [arrays], core_ids=[0])
    return r.results[0]["out_dram"]
```
